# Optimizing a Trainium2 kernel written in Bass

```python
import jax, jax.numpy as jnp
from jax import lax
import numpy as np

D_MODEL = 1024
BATCH = 1
SEQ = 128
DEPTH = 2
DEC_BATCH = 1
DEC_SEQ = 512
PAST_LEN = 256

GRID_W = 64
EPS = 1e-6
ROPE_THETA = 10000.0
BLOCK = 128
N_BRANCH = 3
A_HEADS = 8
A_NOPE = 64
A_ROPE = 32
A_QK = A_NOPE + A_ROPE
A_V = 64
Q_LORA = 384
KV_LORA = 256
B_GROUPS = 8
B_WIDTH = 512
B_CHUNK = 128
C_HEADS = 8
C_KV_HEADS = 2
C_GROUP = C_HEADS // C_KV_HEADS
C_HEAD_DIM = 64
WINDOW = 128
P_HEADS = 8
N_KEYS = 128
N_EXPERTS = N_KEYS * N_KEYS
P_QDIM = 256
P_TOPK = 16
TOKEN_BLOCK = 128
IN_SIZES = (Q_LORA, KV_LORA, A_ROPE, 2 * B_WIDTH, C_HEADS * C_HEAD_DIM,
            C_KV_HEADS * C_HEAD_DIM, C_KV_HEADS * C_HEAD_DIM, N_BRANCH * D_MODEL)
IN_DIM = sum(IN_SIZES)
IN_OFFSETS = tuple(sum(IN_SIZES[:i + 1]) for i in range(len(IN_SIZES) - 1))

kernel_name = 'hybrid_diffusion_prefix_trunk_step'

def rmsnorm(x, g):
    xf = x.astype(jnp.float32)
    y = xf * lax.rsqrt(jnp.mean(xf * xf, axis=-1, keepdims=True) + EPS)
    return (y * g.astype(jnp.float32)).astype(x.dtype)

def axial_rope(n_tokens, dim):
    rows = n_tokens // GRID_W
    row = jnp.repeat(jnp.arange(rows, dtype=jnp.float32), GRID_W)
    col = jnp.tile(jnp.arange(GRID_W, dtype=jnp.float32), rows)
    quarter = dim // 4
    inv_freq = ROPE_THETA ** (-jnp.arange(quarter, dtype=jnp.float32) / quarter)
    ang = jnp.concatenate([row[:, None] * inv_freq, col[:, None] * inv_freq], axis=-1)
    return jnp.cos(ang), jnp.sin(ang)

def apply_rope(x, cos, sin):
    half = x.shape[-1] // 2
    shape = (x.shape[1],) + (1,) * (x.ndim - 3) + (half,)
    c, s = cos.reshape(shape), sin.reshape(shape)
    x1, x2 = x[..., :half], x[..., half:]
    return jnp.concatenate([x1 * c - x2 * s, x2 * c + x1 * s], axis=-1).astype(x.dtype)

def softmax_with_sink(s, sink):
    m = jnp.maximum(jnp.max(s, axis=-1, keepdims=True), sink)
    e = jnp.exp(s - m)
    return e / (jnp.sum(e, axis=-1, keepdims=True) + jnp.exp(sink - m))

def dense_attention(q, k, v, sink=None):
    b, sq, hk, g, d = q.shape
    scale = d ** -0.5
    qb = jnp.moveaxis(q.reshape(b, sq // BLOCK, BLOCK, hk, g, d), 1, 0)

    def attend(q_blk):
        s = jnp.einsum('bqhgd,bkhd->bhgqk', q_blk, k).astype(jnp.float32) * scale
        if sink is None:
            p = jax.nn.softmax(s, axis=-1)
        else:
            p = softmax_with_sink(s, sink.astype(jnp.float32)[None, :, :, None, None])
        return jnp.einsum('bhgqk,bkhd->bqhgd', p.astype(v.dtype), v)

    o = lax.map(attend, qb)
    return jnp.moveaxis(o, 0, 1).reshape(b, sq, hk, g, v.shape[-1])

def windowed_attention(q, k, v, k_ctx, v_ctx, sink):
    b, s, hk, g, d = q.shape
    nb = s // BLOCK
    scale = d ** -0.5
    qb = q.reshape(b, nb, BLOCK, hk, g, d)

    def bands(t):
        tp = jnp.pad(t, ((0, 0), (BLOCK, BLOCK), (0, 0), (0, 0)))
        blk = tp.reshape(b, nb + 2, BLOCK, hk, t.shape[-1])
        return jnp.concatenate([blk[:, :-2], blk[:, 1:-1], blk[:, 2:]], axis=2)

    kb, vb = bands(k), bands(v)
    s_loc = jnp.einsum('bnqhgd,bnkhd->bnhgqk', qb, kb).astype(jnp.float32) * scale
    qpos = jnp.arange(nb)[:, None] * BLOCK + jnp.arange(BLOCK)[None, :]
    kpos = jnp.arange(nb)[:, None] * BLOCK - BLOCK + jnp.arange(3 * BLOCK)[None, :]
    valid = ((jnp.abs(qpos[:, :, None] - kpos[:, None, :]) <= WINDOW)
             & (kpos >= 0)[:, None, :] & (kpos < s)[:, None, :])
    s_loc = jnp.where(valid[None, :, None, None], s_loc, jnp.finfo(jnp.float32).min)
    s_ctx = jnp.einsum('bnqhgd,blhd->bnhgql', qb, k_ctx).astype(jnp.float32) * scale
    p = softmax_with_sink(jnp.concatenate([s_loc, s_ctx], axis=-1),
                          sink.astype(jnp.float32)[None, None, :, :, None, None])
    p = p.astype(v.dtype)
    o = (jnp.einsum('bnhgqk,bnkhd->bnqhgd', p[..., :3 * BLOCK], vb)
         + jnp.einsum('bnhgql,blhd->bnqhgd', p[..., 3 * BLOCK:], v_ctx))
    return o.reshape(b, s, hk, g, d)

def mla_keys_values(ckv_n, krope, w_ukv, g_k):
    b, s, _ = ckv_n.shape
    kv = (ckv_n @ w_ukv).reshape(b, s, A_HEADS, A_NOPE + A_V)
    k_nope, v = kv[..., :A_NOPE], kv[..., A_NOPE:]
    k_rope = jnp.broadcast_to(krope[:, :, None, :], (b, s, A_HEADS, A_ROPE))
    return rmsnorm(jnp.concatenate([k_nope, k_rope], axis=-1), g_k), v

def rope_tail(x, cos, sin):
    return jnp.concatenate([x[..., :A_NOPE], apply_rope(x[..., A_NOPE:], cos, sin)], axis=-1)

def chunk_mlp(z, g_v, w_s, b_s):
    z = jax.nn.gelu(z)
    u, v = z[..., :B_WIDTH], z[..., B_WIDTH:]
    v = rmsnorm(v, g_v)
    b, s, _ = v.shape
    vc = v.reshape(b, s // B_CHUNK, B_CHUNK, B_GROUPS, B_WIDTH // B_GROUPS)
    vm = jnp.einsum('gpq,bnqgc->bnpgc', w_s, vc) + b_s.T[None, None, :, :, None]
    return u * vm.reshape(b, s, B_WIDTH)

def peer(h, w_pq, keys, u_tab, v_tab):
    b, s, d = h.shape
    hb_all = h.reshape(-1, TOKEN_BLOCK, d)

    def one(hb):
        t = hb.shape[0]
        q = (hb @ w_pq).reshape(t, P_HEADS, 2, P_QDIM // 2)
        sc = jnp.einsum('thpd,hpkd->thpk', q, keys).astype(jnp.float32)
        sv, si = lax.top_k(sc, P_TOPK)
        cand = (sv[:, :, 0, :, None] + sv[:, :, 1, None, :]).reshape(t, P_HEADS, P_TOPK * P_TOPK)
        cidx = (si[:, :, 0, :, None] * N_KEYS + si[:, :, 1, None, :]).reshape(t, P_HEADS, P_TOPK * P_TOPK)
        cv, ci = lax.top_k(cand, P_TOPK)
        eidx = jnp.take_along_axis(cidx, ci, axis=-1)
        gate = jax.nn.softmax(cv, axis=-1)
        act = jax.nn.gelu(jnp.einsum('thkd,td->thk', u_tab[eidx], hb).astype(jnp.float32))
        return jnp.einsum('thk,thkd->td', (gate * act).astype(hb.dtype), v_tab[eidx])

    return lax.map(one, hb_all).reshape(b, s, d)

def branches(h, lw, rope, ctx_cache):
    b, s, _ = h.shape
    cq, ckv, krope, zb, qc, kc, vc, gate_logits = jnp.split(h @ lw['w_in'], IN_OFFSETS, axis=-1)
    ckv = rmsnorm(ckv, lw['g_kv_lora'])
    qa = rmsnorm((rmsnorm(cq, lw['g_q_lora']) @ lw['w_uq']).reshape(b, s, A_HEADS, A_QK), lw['g_qk_a_q'])
    ka, va = mla_keys_values(ckv, krope, lw['w_ukv'], lw['g_qk_a_k'])
    qc = rmsnorm(qc.reshape(b, s, C_KV_HEADS, C_GROUP, C_HEAD_DIM), lw['g_qk_c_q'])
    kc = rmsnorm(kc.reshape(b, s, C_KV_HEADS, C_HEAD_DIM), lw['g_qk_c_k'])
    vc = vc.reshape(b, s, C_KV_HEADS, C_HEAD_DIM)
    sink = lw['sink_c'].reshape(C_KV_HEADS, C_GROUP)
    if ctx_cache is None:
        oa = dense_attention(qa[:, :, :, None], ka, va)
        oc = dense_attention(qc, kc, vc, sink)
        new_ctx = (ckv, krope, kc, vc)
    else:
        cos_a, sin_a, cos_c, sin_c = rope
        ctx_ckv, ctx_krope, ctx_k, ctx_v = ctx_cache
        ka_ctx, va_ctx = mla_keys_values(ctx_ckv, ctx_krope, lw['w_ukv'], lw['g_qk_a_k'])
        qa = rope_tail(qa, cos_a, sin_a)
        ka = rope_tail(ka, cos_a, sin_a)
        oa = dense_attention(qa[:, :, :, None], jnp.concatenate([ka, ka_ctx], axis=1),
                             jnp.concatenate([va, va_ctx], axis=1))
        oc = windowed_attention(apply_rope(qc, cos_c, sin_c), apply_rope(kc, cos_c, sin_c), vc,
                                ctx_k, ctx_v, sink)
        new_ctx = None
    ob = chunk_mlp(zb, lw['g_v_b'], lw['w_s_b'], lw['b_s_b'])
    gates = jax.nn.sigmoid(gate_logits.reshape(b, s, N_BRANCH, D_MODEL))
    merged = (gates[:, :, 0] * (oa.reshape(b, s, A_HEADS * A_V) @ lw['w_o_a'])
              + gates[:, :, 1] * (ob @ lw['w_o_b'])
              + gates[:, :, 2] * (oc.reshape(b, s, C_HEADS * C_HEAD_DIM) @ lw['w_o_c']))
    return merged @ lw['w_out'], new_ctx

def layer(x, cond, lw, rope, ctx_cache):
    sh1, sc1, g1, sh2, sc2, g2 = jnp.split(jax.nn.silu(cond) @ lw['w_mod'] + lw['b_mod'], 6, axis=-1)
    h = rmsnorm(x, lw['g_attn_norm']) * (1 + sc1) + sh1
    mix, new_ctx = branches(h, lw, rope, ctx_cache)
    x = x + g1 * mix
    h = rmsnorm(x, lw['g_ffn_norm']) * (1 + sc2) + sh2
    x = x + g2 * peer(h, lw['w_pq'], lw['peer_keys'], lw['peer_u'], lw['peer_v'])
    return x, new_ctx

def setup_inputs(seed: int = 0) -> dict:
    key = jax.random.key(seed)
    keys = jax.random.split(key, 40)
    counter = iter(range(40))
    f32 = jnp.float32
    L, D = DEPTH, D_MODEL

    def nrm(shape, scale=1.0):
        return jax.random.normal(keys[next(counter)], shape, f32) * scale

    def gain(shape):
        return 1.0 + 0.02 * jax.random.normal(keys[next(counter)], shape, f32)

    return {
        'x_prompt': nrm((BATCH, SEQ, D)),
        'x_sample': nrm((DEC_BATCH, DEC_SEQ, D)),
        'c': nrm((DEC_BATCH, D)),
        'cache_mla_ckv': nrm((DEC_BATCH, L, PAST_LEN, KV_LORA)),
        'cache_mla_krope': nrm((DEC_BATCH, L, PAST_LEN, A_ROPE)),
        'cache_swa_k': nrm((DEC_BATCH, L, PAST_LEN, C_KV_HEADS, C_HEAD_DIM)),
        'cache_swa_v': nrm((DEC_BATCH, L, PAST_LEN, C_KV_HEADS, C_HEAD_DIM)),
        'c_ctx': nrm((D,)),
        'w_mod': nrm((L, D, 6 * D), D ** -0.5),
        'b_mod': nrm((L, 6 * D), 0.02),
        'g_attn_norm': gain((L, D)),
        'w_in': nrm((L, D, IN_DIM), D ** -0.5),
        'g_q_lora': gain((L, Q_LORA)),
        'w_uq': nrm((L, Q_LORA, A_HEADS * A_QK), Q_LORA ** -0.5),
        'g_kv_lora': gain((L, KV_LORA)),
        'w_ukv': nrm((L, KV_LORA, A_HEADS * (A_NOPE + A_V)), KV_LORA ** -0.5),
        'g_qk_a_q': gain((L, A_QK)),
        'g_qk_a_k': gain((L, A_QK)),
        'w_o_a': nrm((L, A_HEADS * A_V, D), (A_HEADS * A_V) ** -0.5),
        'g_v_b': gain((L, B_WIDTH)),
        'w_s_b': nrm((L, B_GROUPS, B_CHUNK, B_CHUNK), B_CHUNK ** -0.5),
        'b_s_b': gain((L, B_GROUPS, B_CHUNK)),
        'w_o_b': nrm((L, B_WIDTH, D), B_WIDTH ** -0.5),
        'g_qk_c_q': gain((L, C_HEAD_DIM)),
        'g_qk_c_k': gain((L, C_HEAD_DIM)),
        'sink_c': nrm((L, C_HEADS), 0.5),
        'w_o_c': nrm((L, C_HEADS * C_HEAD_DIM, D), (C_HEADS * C_HEAD_DIM) ** -0.5),
        'w_out': nrm((L, D, D), D ** -0.5),
        'g_ffn_norm': gain((L, D)),
        'w_pq': nrm((L, D, P_HEADS * P_QDIM), D ** -0.5),
        'peer_keys': nrm((L, P_HEADS, 2, N_KEYS, P_QDIM // 2), (P_QDIM // 2) ** -0.5),
        'peer_u': nrm((L, N_EXPERTS, D), D ** -0.5),
        'peer_v': nrm((L, N_EXPERTS, D), P_HEADS ** -0.5),
    }

def reference(x_prompt, x_sample, c, cache_mla_ckv, cache_mla_krope, cache_swa_k, cache_swa_v, c_ctx,
              w_mod, b_mod, g_attn_norm, w_in, g_q_lora, w_uq, g_kv_lora, w_ukv, g_qk_a_q, g_qk_a_k,
              w_o_a, g_v_b, w_s_b, b_s_b, w_o_b, g_qk_c_q, g_qk_c_k, sink_c, w_o_c, w_out, g_ffn_norm,
              w_pq, peer_keys, peer_u, peer_v):
    n_lat = x_sample.shape[1]
    rope = axial_rope(n_lat, A_ROPE) + axial_rope(n_lat, C_HEAD_DIM)
    ctx_cond = c_ctx[None, None, :]
    lat_cond = c[:, None, :]
    y_prompt, y_sample = x_prompt, x_sample
    ckv_list, krope_list, k_list, v_list = [], [], [], []
    for l in range(DEPTH):
        lw = {
            'w_mod': w_mod[l], 'b_mod': b_mod[l], 'g_attn_norm': g_attn_norm[l], 'w_in': w_in[l],
            'g_q_lora': g_q_lora[l], 'w_uq': w_uq[l], 'g_kv_lora': g_kv_lora[l], 'w_ukv': w_ukv[l],
            'g_qk_a_q': g_qk_a_q[l], 'g_qk_a_k': g_qk_a_k[l], 'w_o_a': w_o_a[l], 'g_v_b': g_v_b[l],
            'w_s_b': w_s_b[l], 'b_s_b': b_s_b[l], 'w_o_b': w_o_b[l], 'g_qk_c_q': g_qk_c_q[l],
            'g_qk_c_k': g_qk_c_k[l], 'sink_c': sink_c[l], 'w_o_c': w_o_c[l], 'w_out': w_out[l],
            'g_ffn_norm': g_ffn_norm[l], 'w_pq': w_pq[l], 'peer_keys': peer_keys[l],
            'peer_u': peer_u[l], 'peer_v': peer_v[l],
        }
        y_prompt, (ckv_l, krope_l, k_l, v_l) = layer(y_prompt, ctx_cond, lw, None, None)
        ckv_list.append(ckv_l)
        krope_list.append(krope_l)
        k_list.append(k_l)
        v_list.append(v_l)
        ctx_cache = (cache_mla_ckv[:, l], cache_mla_krope[:, l], cache_swa_k[:, l], cache_swa_v[:, l])
        y_sample, _ = layer(y_sample, lat_cond, lw, rope, ctx_cache)
    new_mla_ckv = jnp.stack(ckv_list, axis=1)
    new_mla_krope = jnp.stack(krope_list, axis=1)
    new_swa_k = jnp.stack(k_list, axis=1)
    new_swa_v = jnp.stack(v_list, axis=1)
    return (y_prompt, y_sample, new_mla_ckv, new_mla_krope, new_swa_k, new_swa_v)


_drawn_inputs = setup_inputs


def setup_inputs(seed=0):
    import zlib

    import numpy as np

    out = dict(_drawn_inputs(seed))
    spreads = {}
    factors = {'cache_mla_krope': 3.046,
     'g_q_lora': 8.0,
     'g_kv_lora': 2.932,
     'g_qk_a_q': 8.0,
     'g_qk_a_k': 8.0,
     'g_v_b': 3.384,
     'b_s_b': 3.232,
     'g_qk_c_q': 8.0,
     'g_qk_c_k': 2.955,
     'sink_c': 55.168,
     'cache_swa_k': 3.11,
     'cache_swa_v': 3.986}
    for name, (base, spread) in spreads.items():
        noise = np.random.default_rng([zlib.crc32(name.encode()), seed]).standard_normal(out[name].shape)
        drawn = base * np.exp(spread * noise) if base else spread * noise
        out[name] = __import__('jax').numpy.asarray(drawn.astype(out[name].dtype))
    for name, factor in factors.items():
        out[name] = (out[name] * factor).astype(out[name].dtype)
    return out
```

```python
from contextlib import ExitStack

import concourse.bass as bass
from concourse import mybir

ALU = mybir.AluOpType
ACT = mybir.ActivationFunctionType
AX = mybir.AxisListType
F32 = mybir.dt.float32
U32 = mybir.dt.uint32

P = 128
D = 1024
L = 2
NT = 5
NKT = NT + 2
DK = D // P
EPS = 1e-6
H = 8
NOPE, ROPE, AQK = 64, 32, 96
QL, KVL = 384, 256
CD, CKV = 64, 2
TOPK = 16
NEXP = 128 * 128
SLOTS = H * TOPK
NEG = -1e30
LOW = -3.0e38

GAINS = {}
_at = 0
for _n, _s in (("kv", KVL), ("q", QL), ("qa", AQK), ("ka", AQK), ("v", 512), ("qc", CD), ("kc", CD), ("sink", H)):
    GAINS[_n] = (_at, _s)
    _at += _s
NG = _at

UNIT = 2048
NU = 5
UNITS = ([(("mod", b, k), 2048) for b in range(12) for k in range(2)]
         + [(("kv", 0, k), 4 * 288) for k in range(2)]
         + [(("cq", 0, k), 4 * 384) for k in range(2)]
         + [(("ukv", 0, 0), 2048)]
         + [(("u", 0, k), 2048) for k in range(2)]
         + [(("uq", 0, k), 3 * 384) for k in range(2)]
         + [(("v", 0, k), 2048) for k in range(2)]
         + [(("ws", 0, 0), 1024)]
         + [(("qc", 0, k), 2048) for k in range(2)]
         + [(("kc", 0, k), 1024) for k in range(2)]
         + [((n, 2 * b + c, k), 2048) for b in range(3) for c in range(2) for n, k in (("gate", 0), ("gate", 1), ("proj", 0))]
         + [(("out", c, k), 2048) for c in range(2) for k in range(2)]
         + [(("pq", q, 0), 2048) for q in range(8)])
UNO = {}
_at = 0
for _i, (_n, _s) in enumerate(UNITS):
    UNO[_n] = (_i, _at, _s)
    _at += P * _s
WTOTAL = _at


def tensor_steps():
    s = [("mod", b) for b in range(12)]
    s += [("hT", 0, i) for i in range(NT)]
    s += [("kv", i) for i in range(NT)] + [("cq", i) for i in range(NT)]
    for i in range(NKT):
        s += [("ckvT", i)] if i < NT else []
        s += [("ukv", i, 0), ("ukv", i, 1)]
        s += [("kaT", i - 1)] if i else []
    s += [("kaT", NKT - 1)]
    s += [("u", i) for i in range(NT)]
    for i in range(NT):
        s += [("cqT", i), ("uq", i, 0), ("uq", i, 1)]
    s += [("v", i) for i in range(NT)]
    s += [("vm", i) for i in range(NT)]
    s += [("qc", i) for i in range(NT)] + [("kc", i) for i in range(NT)] + [("kcT", i) for i in range(NT)]
    n = 2 * H * NT
    s += [("qT", 0)]
    for u in range(n + 2):
        if u < n:
            s += [("s", u)]
        if 1 <= u <= n:
            s += [("PT", u - 1)]
        if u % H == 5 and u + 3 < n:
            s += [("qT", u // H + 1)]
        if u >= 2:
            s += [("O", u - 2)]
            if u - 2 > 2 * H and (u - 2) % (2 * H) == 1:
                s += [("oT", (u - 2) // (2 * H) - 1, j) for j in range(2)]
    s += [("oT", NT - 1, j) for j in range(2)]
    for bc in range(6):
        for i in range(NT):
            s += [("g", bc, i), ("p", bc, i)]
    for i in range(NT):
        s += [("mT", i), ("o", i, 0), ("o", i, 1)]
    s += [("hT", 1, i) for i in range(NT)]
    s += [("pq", q) for q in range(16)]
    return s


STEPS = tensor_steps()
ONE = ("mod", "kv", "cq", "ukv", "u", "uq", "v", "vm", "qc", "kc", "g", "p", "o")
TWO = ("hT", "ckvT", "kaT", "cqT", "kcT", "qT", "s", "PT", "oT", "mT", "pq")
ONES = [s for s in STEPS if s[0] in ONE]
PAIRS = [s for s in STEPS if s[0] in TWO]
ONE_NO = {s: j for j, s in enumerate(ONES)}
PAIR_NO = {s: j for j, s in enumerate(PAIRS)}
NB1, NB2 = 2, 3

LAST_USE = {}
for _n in UNO:
    LAST_USE[_n] = {"mod": lambda b: ("mod", b), "kv": lambda b: ("kv", 4), "cq": lambda b: ("cq", 4),
                    "ukv": lambda b: ("ukv", NKT - 1, 1), "u": lambda b: ("u", 4), "uq": lambda b: ("uq", 4, 1),
                    "v": lambda b: ("v", 4), "ws": lambda b: ("vm", 4), "qc": lambda b: ("qc", 4),
                    "kc": lambda b: ("kc", 4), "gate": lambda b: ("p", b, 4), "proj": lambda b: ("p", b, 4),
                    "out": lambda b: ("o", 4, 1), "pq": lambda b: ("pq", 2 * b + 1)}[_n[0]](_n[1])

NORMS = ([(("n", 0), NT, D)] + [(("ckv", i), 1, KVL) for i in range(NT)] + [(("cq", i), 1, QL) for i in range(NT)]
         + [(("ka", i), H, AQK) for i in range(NKT)] + [(("qa", i), H, AQK) for i in range(NT)]
         + [(("v", i), 1, 512) for i in range(NT)]
         + [(("qc", i), H, CD) for i in range(NT)] + [(("kc", i), CKV, CD) for i in range(NT)] + [(("n", 1), NT, D)])
NORM_AT = {}
_at = 0
for _i, (_k, _c, _w) in enumerate(NORMS):
    NORM_AT[_k] = (_i, _at, _c, _w)
    _at += _c
NSTAT = _at


def a_keys(i):
    return [0] if i == 0 else list(range(1, NKT))


def c_keys(i):
    return [0] if i == 0 else [NT, NT + 1] + [t for t in (i - 1, i, i + 1) if 1 <= t < NT]


def unit_keys(u):
    i, r = divmod(u, 2 * H)
    return a_keys(i) if r < H else c_keys(i)


RING = 8
GRP = 4
BODY = 32
TURNS = SLOTS // BODY
NGRP = BODY // GRP


class Signal:

    def __init__(self, sem, layer):
        self.sem, self.layer = sem, layer

    def at(self, l, n):
        return l * self.layer + n


def build(nc, ins, outs):
    with ExitStack() as ctx:
        sb = lambda n, s, d=F32: ctx.enter_context(nc.sbuf_tensor(n, s, d))

        def signal(name, layer):
            return Signal(ctx.enter_context(nc.semaphore(name)), layer)

        x = sb("x", [P, NT, D])
        z = sb("z", [P, NT, 1792])
        kcv = sb("kcv", [P, 2688])
        big = sb("big", [P, 7168 + 3584])
        arena = sb("arena", [P, NU * UNIT + NT * D + 6240])
        sq = sb("sq", [P, D])
        ident = sb("ident", [P, P])
        zeros = sb("zeros", [P, P])
        ones = sb("ones", [1, P])
        mask = sb("mask", [P, 2, P])
        rope = sb("rope", [P, 4, 96])
        gains = sb("gains", [P, NG])
        bs = sb("bs", [P, H])
        cond = sb("cond", [P, DK, 2])
        ss = sb("ss", [P, NSTAT])
        rstd = sb("rstd", [P, NSTAT])
        negm = sb("negm", [P, 2 * H * NT])
        rsum = sb("rsum", [P, 2 * H * NT])
        base = sb("base", [P, 1])
        mhalf = sb("mhalf", [P, 1])

        wring = [arena[:, r * UNIT:(r + 1) * UNIT] for r in range(NU)]
        hT = arena[:, NU * UNIT:NU * UNIT + NT * D].rearrange("p (k t) -> p k t", k=DK)
        S0 = NU * UNIT + NT * D
        scr = lambda a, n: arena[:, S0 + a:S0 + a + n]
        hbuf = [scr(0, D), scr(D, D)]
        z0 = [scr(288 * i, 288) for i in range(NT)]
        kr_ctx = scr(1440, 64)
        ckvT_ctx = scr(1504, 512).rearrange("p (k t) -> p k t", k=2)
        zq = [scr(2016 + QL * i, QL) for i in range(NT)]
        kbuf = [scr(3936 + 768 * r, 768) for r in range(2)]
        latT = [scr(5472 + QL * r, QL) for r in range(2)]
        vb = [scr(512 * i, 512) for i in range(NT)]
        kcb = [scr(2560 + 128 * i, 128) for i in range(NT)]
        otok = scr(0, D)
        pb = [scr(1024 + 776 * r, 776) for r in range(2)]
        ptb = [scr(2576 + 768 * r, 768) for r in range(2)]
        qTb = [scr(4112, D), scr(5136, D)]
        sg = [scr(512 * r, 512) for r in range(2)]
        mT = [scr(1024 + D * r, D) for r in range(2)]

        kaT = big[0:AQK, 0:7168].rearrange("p (h t) -> p h t", h=H)
        va = big[:, 7168:].rearrange("p (t n) -> p t n", t=NKT)
        merged = big[:, 0:NT * D].rearrange("p (t n) -> p t n", t=NT)
        g1 = big[:, 5120:7168].rearrange("p (s n) -> p s n", s=2)
        rows = big[:, 0:4096].rearrange("p (s a n) -> p s a n", s=2, a=2)
        grow = big[:, 4096:5120]
        pqT = big[:, 0:16 * NT * P].rearrange("p (q t) -> p q t", q=16)
        kcT = kcv[0:CD, 0:1792].rearrange("p (g t) -> p g t", g=CKV)
        vc = kcv[:, 1792:2688].rearrange("p (t n) -> p t n", t=NKT)
        g2 = kcv[:, 0:2048].rearrange("p (s n) -> p s n", s=2)
        modrow = z[0:2, :, :].rearrange("p t n -> p (t n)")[:, 0:6144]
        zflat = z[:, :, :].rearrange("p t n -> p (t n)")
        h2 = zflat[:, 0:NT * D].rearrange("p (t n) -> p t n", t=NT)
        keys = zflat[:, 5120:7168].rearrange("p (q n) -> p q n", q=16)
        oT = [z[:, i, 0:1536].rearrange("p (k t) -> p k t", k=12) for i in range(NT)]

        ring = [arena[:, r * 2 * D:(r + 1) * 2 * D] for r in range(RING)]
        T0 = RING * 2 * D - S0
        cand = scr(T0, 2048)
        v16 = scr(T0 + 2048, 256)
        i16 = scr(T0 + 2304, 256).bitcast(U32)
        i16f = scr(T0 + 2560, 256)
        tmpk = [zflat[:, 7168 + 256 * r:7168 + 256 * (r + 1)] for r in range(2)]
        cv = zflat[:, 7680:7808]
        ci = zflat[:, 7808:7936].bitcast(U32)
        cab = zflat[:, 7936:8192].bitcast(U32)
        cabf = zflat[:, 8192:8448]
        sel = zflat[:, 8448:8704]
        esum = zflat[:, 8704:8712]
        iota = zflat[:, 8712:8728]
        idx = [scr(T0 + 2816 + 128 * r, 128).bitcast(U32) for r in range(2)]
        gate = [scr(T0 + 3072 + 128 * r, 128) for r in range(2)]
        ihead = scr(T0 + 3328, BODY).bitcast(U32)
        ghead = scr(T0 + 3360, BODY)
        dots = scr(T0 + 3392, BODY)
        gel = scr(T0 + 3424, BODY)
        wts = scr(T0 + 3456, BODY)
        diag = [scr(T0 + 3488 + P * r, P) for r in range(RING)]
        assert T0 + 3488 + RING * P <= 6240

        ps = ctx.enter_context(nc.psum_tensor("ps", [P, 8, 512], F32))
        one = [ps[:, b, :] for b in range(NB1)]
        pair = [ps[:, 2 + 2 * b:4 + 2 * b, :].rearrange("p a n -> p (a n)") for b in range(NB2)]
        acc = [ps[:, 0:2, :].rearrange("p a n -> p (a n)"), pair[2]]
        modd = nc.dram_tensor("mod_rows", [2, 6144], F32, kind="Internal").ap()

        def uses(n, total, b):
            return (total - b + n - 1) // n

        x_in = signal("x_in", 0)
        const_in = signal("const_in", 0)
        cond_in = signal("cond_in", 0)
        cond_ready = signal("cond_ready", 0)
        const_ready = signal("const_ready", 0)
        layer_end = signal("layer_end", 5)
        layer_in = signal("layer_in", 16 * 7)
        w_land = [signal(f"w_land{r}", 16 * uses(NU, len(UNITS), r)) for r in range(NU)]
        one_full = signal("one_full", len(ONES))
        one_free = [signal(f"one_free{b}", uses(NB1, len(ONES), b)) for b in range(NB1)]
        pair_full = signal("pair_full", len(PAIRS))
        pair_free = [signal(f"pair_free{b}", uses(NB2, len(PAIRS), b)) for b in range(NB2)]
        mod_stored = signal("mod_stored", 16)
        mod_ready = signal("mod_ready", 1)
        rows_in = signal("rows_in", 2 * 16 * 5)
        gates_in = signal("gates_in", 16 * 4)
        keys_in = signal("keys_in", 16)
        ss_ready = signal("ss_ready", len(NORMS))
        mid_ready = signal("mid_ready", len(NORMS))
        rstd_ready = signal("rstd_ready", len(NORMS))
        h_ready = signal("h_ready", 2 * NT)
        hT_ready = signal("hT_ready", 2 * NT)
        z0_ready = signal("z0_ready", NT)
        zq_ready = signal("zq_ready", NT)
        ckv_ready = signal("ckv_ready", NT)
        cq_ready = signal("cq_ready", NT)
        ckvT_ready = signal("ckvT_ready", NT)
        cqT_ready = signal("cqT_ready", NT)
        nope_in = signal("nope_in", NKT)
        ka_ready = signal("ka_ready", NKT)
        kaT_ready = signal("kaT_ready", NKT)
        u_in = signal("u_in", NT)
        qa_in = signal("qa_in", 2 * NT)
        qa_ready = signal("qa_ready", NT)
        v_in = signal("v_in", NT)
        v_ready = signal("v_ready", NT)
        ob_ready = signal("ob_ready", NT)
        qc_in = signal("qc_in", NT)
        qc_ready = signal("qc_ready", NT)
        kc_in = signal("kc_in", NT)
        kc_ready = signal("kc_ready", NT)
        kcT_ready = signal("kcT_ready", NT)
        latents_stored = signal("latents_stored", 32)
        kv_stored = signal("kv_stored", 32)
        qT_ready = signal("qT_ready", 2 * NT)
        max_ready = signal("max_ready", 2 * H * NT)
        exp_ready = signal("exp_ready", 2 * H * NT)
        pt_ready = signal("pt_ready", 2 * H * NT)
        o_done = signal("o_done", 2 * H * NT)
        o_moved = signal("o_moved", 2 * NT)
        oT_ready = signal("oT_ready", 2 * NT)
        sg_ready = signal("sg_ready", 6 * NT)
        merge_done = signal("merge_done", 6 * NT)
        mT_ready = signal("mT_ready", NT)
        pq_ready = signal("pq_ready", 16)
        scores_full = signal("scores_full", 2 * NT)
        scores_used = signal("scores_used", 2 * NT)
        cv_ready = signal("cv_ready", NT)
        ce_ready = signal("ce_ready", NT)
        idx_ready = signal("idx_ready", NT)
        head_ready = signal("head_ready", NT * TURNS)
        g_land = [signal(f"g_land{r}", 16 * NT * SLOTS // RING) for r in range(RING)]
        dots_ready = signal("dots_ready", NT * SLOTS // GRP)
        gel_ready = signal("gel_ready", NT * SLOTS // GRP)
        wts_ready = signal("wts_ready", NT * SLOTS // GRP)
        diag_ready = signal("diag_ready", NT * SLOTS)
        slot_used = signal("slot_used", NT * SLOTS + RING)
        acc_full = signal("acc_full", NT)
        acc_used = signal("acc_used", NT)
        y_stored = signal("y_stored", 0)

        waits_passed = signal("waits_passed", 0)

        def alone(eng):
            eng.sem_inc(waits_passed.sem, 1)

        def unit_ap(l, n):
            _, at, size = UNO[n]
            row = ins["weights"][bass.ds(l, 1), at:at + P * size]
            return row.rearrange("a (p n) -> (a p) n", p=P)

        def unit_in(name, k, shape):
            i, _, size = UNO[name]
            return wring[i % NU][:, 0:size].rearrange("p (k n) -> p k n", k=shape)

        def one_of(step):
            return one[ONE_NO[step] % NB1]

        def pair_of(step):
            return pair[PAIR_NO[step] % NB2]

        block = ctx.enter_context(nc.Block())

        @block.sync
        def _(sp):
            for i in range(NT):
                src = ins["x_prompt"][0] if i == 0 else ins["x_sample"][0, (i - 1) * P:i * P, :]
                sp.dma_start(x[:, i, :], src).then_inc(x_in.sem, 16)
            with sp.Fori(0, L) as l:
                for n, (name, size) in enumerate(UNITS):
                    if n >= NU:
                        last = LAST_USE[UNITS[n - NU][0]]
                        if last in ONE_NO:
                            sp.wait_ge(one_full.sem, one_full.at(l, ONE_NO[last] + 1))
                            alone(sp)
                        else:
                            sp.wait_ge(pair_full.sem, pair_full.at(l, PAIR_NO[last] + 1))
                            alone(sp)
                    sp.dma_start(wring[n % NU][:, 0:size], unit_ap(l, name)).then_inc(w_land[n % NU].sem, 16)
                sp.drain().then_inc(layer_end.sem, 1)
                sp.wait_ge(layer_end.sem, layer_end.at(l, 5))
                alone(sp)
            for i in range(NT):
                dst = outs["y_prompt"][0] if i == 0 else outs["y_sample"][0, (i - 1) * P:i * P, :]
                sp.dma_start(dst, x[:, i, :]).then_inc(y_stored.sem, 16)
            sp.wait_ge(y_stored.sem, 16 * NT)

        @block.gpsimd
        def _(pool):
            nc.gpsimd.memset(zeros[:], 0.0)
            nc.gpsimd.memset(mhalf[:], -0.5)
            nc.gpsimd.memset(ones[:], 1.0)
            nc.gpsimd.memset(base[:], 0.0).then_inc(const_ready.sem, 1)
            pool.wait_ge(const_ready.sem, 1)
            alone(pool)
            with pool.Fori(0, L) as l:
                for e, (key, cols, width) in enumerate(NORMS):
                    _, at, _, _ = NORM_AT[key]
                    pool.wait_ge(ss_ready.sem, ss_ready.at(l, e + 1))
                    alone(pool)
                    nc.gpsimd.tensor_scalar(ss[:, at:at + cols], ss[:, at:at + cols], 1.0 / width, EPS,
                                            ALU.mult, ALU.add).then_inc(mid_ready.sem, 1)
                    pool.wait_ge(mid_ready.sem, mid_ready.at(l, e + 1))
                    alone(pool)
                    nc.gpsimd.tensor_tensor(rstd[:, at:at + cols], ss[:, at:at + cols],
                                            mhalf[:].to_broadcast([P, cols]), ALU.pow).then_inc(rstd_ready.sem, 1)
                pool.wait_ge(pair_full.sem, pair_full.at(l, len(PAIRS)))
                alone(pool)
                for i in range(NT):
                    with pool.Fori(0, TURNS) as t:
                        pool.wait_ge(head_ready.sem, l * head_ready.layer + t + (i * TURNS + 1))
                        alone(pool)
                        for s in range(BODY):
                            pool.wait_ge(slot_used.sem, l * slot_used.layer + t * BODY + (i * SLOTS + s + 1))
                            alone(pool)
                            pool.indirect_dma_start(
                                out=ring[s % RING], out_offset=None, in_=ins["experts"],
                                in_offset=bass.IndirectOffsetOnAxis(ap=ihead[:, s:s + 1], axis=0)
                            ).then_inc(g_land[s % RING].sem, 16)
                pool.drain().then_inc(layer_end.sem, 1)
                pool.wait_ge(layer_end.sem, layer_end.at(l, 5))
                alone(pool)

        @block.tensor
        def _(pe):
            MM = nc.tensor.matmul
            TR = nc.tensor.transpose

            pe.wait_ge(cond_ready.sem, 2)
            pe.wait_ge(const_in.sem, 16 * 3)
            pe.wait_ge(const_ready.sem, 1)
            with pe.Fori(0, L) as l:
                landed = set()

                def unit(name, k):
                    n = UNO[name][0]
                    if name not in landed:
                        landed.add(name)
                        pe.wait_ge(w_land[n % NU].sem, w_land[n % NU].at(l, 16 * (n // NU + 1)))
                    return unit_in(name, 0, k)

                def project(dst, i, name, cols):
                    for k in range(DK):
                        w = unit((name[0], name[1], k // 4), 4)
                        last = MM(dst[:, 0:cols], hT[:, k, i * P:(i + 1) * P], w[:, k % 4, :], start=k == 0, stop=k == DK - 1)
                    return last

                for step in STEPS:
                    kind, i = step[0], step[1]
                    if step in ONE_NO:
                        j = ONE_NO[step]
                        if j >= NB1:
                            pe.wait_ge(one_free[j % NB1].sem, one_free[j % NB1].at(l, j // NB1))
                        dst = one_of(step)
                    elif step in PAIR_NO:
                        j = PAIR_NO[step]
                        if j >= NB2:
                            pe.wait_ge(pair_free[j % NB2].sem, pair_free[j % NB2].at(l, j // NB2))
                        dst = pair_of(step)

                    if kind == "mod":
                        for k in range(DK):
                            w = unit(("mod", i, k // 4), 4)
                            last = MM(dst[0:2, :], cond[:, k, :], w[:, k % 4, :], start=k == 0, stop=k == DK - 1)
                        last.then_inc(one_full.sem, 1)
                    elif kind == "hT":
                        phase, i = step[1:]
                        pe.wait_ge(h_ready.sem, h_ready.at(l, phase * NT + i + 1))
                        src = h2[:, i, :] if phase else hbuf[i % 2]
                        for k in range(DK):
                            last = TR(dst[:, k * P:(k + 1) * P], src[:, k * P:(k + 1) * P], ident[:])
                        last.then_inc(pair_full.sem, 1)
                    elif kind in ("kv", "cq", "u", "v", "qc", "kc"):
                        if kind == "kv":
                            pe.wait_ge(hT_ready.sem, hT_ready.at(l, i + 1))
                        cols = {"kv": 288, "cq": QL, "kc": 256}.get(kind, 512)
                        project(dst, i, (kind, 0), cols).then_inc(one_full.sem, 1)
                    elif kind == "ckvT":
                        pe.wait_ge(ckv_ready.sem, ckv_ready.at(l, i + 1))
                        for k in range(2):
                            last = TR(dst[:, k * P:(k + 1) * P], z0[i][:, k * P:(k + 1) * P], ident[:])
                        last.then_inc(pair_full.sem, 1)
                    elif kind == "ukv":
                        half = step[2]
                        if i < NT:
                            pe.wait_ge(ckvT_ready.sem, ckvT_ready.at(l, i + 1))
                            src = latT[i % 2].rearrange("p (k t) -> p k t", k=3)
                        else:
                            pe.wait_ge(layer_in.sem, layer_in.at(l, layer_in.layer))
                            src = ckvT_ctx[:, :, (i - NT) * P:(i - NT + 1) * P]
                        w = unit(("ukv", 0, 0), 2)
                        for k in range(2):
                            last = MM(dst, src[:, k, :], w[:, k, half * 512:(half + 1) * 512], start=k == 0, stop=k == 1)
                        last.then_inc(one_full.sem, 1)
                    elif kind == "kaT":
                        pe.wait_ge(ka_ready.sem, ka_ready.at(l, i + 1))
                        for h in range(H):
                            last = TR(dst[0:AQK, h * P:(h + 1) * P], kbuf[i % 2][:, h * AQK:(h + 1) * AQK], ident[:])
                        last.then_inc(pair_full.sem, 1)
                    elif kind == "cqT":
                        pe.wait_ge(cq_ready.sem, cq_ready.at(l, i + 1))
                        for k in range(3):
                            last = TR(dst[:, k * P:(k + 1) * P], zq[i][:, k * P:(k + 1) * P], ident[:])
                        last.then_inc(pair_full.sem, 1)
                    elif kind == "uq":
                        pe.wait_ge(cqT_ready.sem, cqT_ready.at(l, i + 1))
                        w = unit(("uq", 0, step[2]), 3)
                        for k in range(3):
                            last = MM(dst[:, 0:384], latT[i % 2][:, k * P:(k + 1) * P], w[:, k, :], start=k == 0, stop=k == 2)
                        last.then_inc(one_full.sem, 1)
                    elif kind == "vm":
                        pe.wait_ge(v_ready.sem, v_ready.at(l, i + 1))
                        w = unit(("ws", 0, 0), H)
                        for g in range(H):
                            last = MM(dst[:, g * 64:(g + 1) * 64], w[:, g, :], vb[i][:, g * 64:(g + 1) * 64], start=True, stop=True)
                        last.then_inc(one_full.sem, 1)
                    elif kind == "kcT":
                        pe.wait_ge(kc_ready.sem, kc_ready.at(l, i + 1))
                        alone(pe)
                        for g in range(CKV):
                            last = TR(dst[0:CD, g * P:(g + 1) * P], kcb[i][:, g * CD:(g + 1) * CD], ident[:])
                        last.then_inc(pair_full.sem, 1)
                    elif kind == "qT":
                        t, m = divmod(i, 2)
                        if m == 0:
                            pe.wait_ge(qa_ready.sem, qa_ready.at(l, t + 1))
                            src, w = z[:, t, 1024:1792], AQK
                        else:
                            pe.wait_ge(qc_ready.sem, qc_ready.at(l, t + 1))
                            alone(pe)
                            src, w = z[:, t, 512:1024], CD
                        for h in range(H):
                            last = TR(dst[0:w, h * P:(h + 1) * P], src[:, h * w:(h + 1) * w], ident[:])
                        last.then_inc(pair_full.sem, 1)
                    elif kind == "s":
                        t, r = divmod(i, 2 * H)
                        m, h = divmod(r, H)
                        ks = unit_keys(i)
                        w, kT, g = (AQK, kaT, h) if m == 0 else (CD, kcT, h // (H // CKV))
                        if h == 0:
                            pe.wait_ge(qT_ready.sem, qT_ready.at(l, 2 * t + m + 1))
                        if i == 0:
                            pe.wait_ge(kaT_ready.sem, kaT_ready.at(l, NKT))
                        if i == H:
                            pe.wait_ge(kcT_ready.sem, kcT_ready.at(l, NT))
                            pe.wait_ge(layer_in.sem, layer_in.at(l, layer_in.layer))
                        q = qTb[m].rearrange("p (h t) -> p h t", h=H)[0:w, h, :]
                        c = 0
                        while c < len(ks):
                            n = 1
                            while c + n < len(ks) and ks[c + n] == ks[c] + n and (c + n) % 4:
                                n += 1
                            masks = [(c + d, int(ks[c + d] > t)) for d in range(n) if m and t and ks[c + d] < NT and ks[c + d] != t]
                            last = MM(dst[:, c * P:(c + n) * P], q, kT[:, g, ks[c] * P:(ks[c] + n) * P], start=True, stop=not masks)
                            for e, (pos, side) in enumerate(masks):
                                last = MM(dst[:, pos * P:(pos + 1) * P], ident[:], mask[:, side, :], start=False, stop=e == len(masks) - 1)
                            c += n
                        if m:
                            a = GAINS["sink"][0] + h
                            last = MM(dst[:, len(ks) * P:len(ks) * P + 1], ones[:], gains[0:1, a:a + 1], start=True, stop=True)
                        last.then_inc(pair_full.sem, 1)
                    elif kind == "PT":
                        pe.wait_ge(exp_ready.sem, exp_ready.at(l, i + 1))
                        for k in range(len(unit_keys(i))):
                            last = TR(dst[:, k * P:(k + 1) * P], pb[i % 2][:, k * P:(k + 1) * P], ident[:])
                        last.then_inc(pair_full.sem, 1)
                    elif kind == "O":
                        t, r = divmod(i, 2 * H)
                        m, h = divmod(r, H)
                        if i == 0:
                            for b in range(NB1):
                                n = sum(1 for s in ONES[:ONE_NO[("g", 0, 0)]] if ONE_NO[s] % NB1 == b)
                                pe.wait_ge(one_free[b].sem, one_free[b].at(l, n))
                        if h == 0 and t:
                            pe.wait_ge(o_moved.sem, o_moved.at(l, 2 * (t - 1) + m + 1))
                        pe.wait_ge(pt_ready.sem, pt_ready.at(l, i + 1))
                        ks = unit_keys(i)
                        for k, kt in enumerate(ks):
                            v = va[:, kt, h * 64:(h + 1) * 64] if m == 0 else vc[:, kt, h // (H // CKV) * CD:(h // (H // CKV) + 1) * CD]
                            last = MM(one[m][:, h * 64:(h + 1) * 64], ptb[i % 2][:, k * P:(k + 1) * P], v, start=k == 0, stop=k == len(ks) - 1)
                        last.then_inc(o_done.sem, 1)
                    elif kind == "oT":
                        pe.wait_ge(o_moved.sem, o_moved.at(l, 2 * i + 2))
                        if step[2] == 0:
                            pe.wait_ge(ob_ready.sem, ob_ready.at(l, i + 1))
                            blocks = [otok[:, k * P:(k + 1) * P] for k in range(4)] + [z[:, i, k * P:(k + 1) * P] for k in range(4)]
                        else:
                            blocks = [otok[:, 512 + k * P:512 + (k + 1) * P] for k in range(4)]
                        for k, src in enumerate(blocks):
                            last = TR(dst[:, k * P:(k + 1) * P], src, ident[:])
                        last.then_inc(pair_full.sem, 1)
                    elif kind == "g":
                        t = step[2]
                        if step == ("g", 0, 0):
                            pe.wait_ge(o_moved.sem, o_moved.at(l, 2 * NT))
                        project(dst, t, ("gate", i), 512).then_inc(one_full.sem, 1)
                    elif kind == "p":
                        t, b = step[2], i // 2
                        if i == 0:
                            pe.wait_ge(oT_ready.sem, oT_ready.at(l, 2 * t + 2))
                        w = unit(("proj", i, 0), 4)
                        for k in range(4):
                            last = MM(dst, oT[t][:, 4 * b + k, :], w[:, k, :], start=k == 0, stop=k == 3)
                        last.then_inc(one_full.sem, 1)
                    elif kind == "mT":
                        pe.wait_ge(merge_done.sem, merge_done.at(l, 5 * NT + i + 1))
                        for k in range(DK):
                            last = TR(dst[:, k * P:(k + 1) * P], merged[:, i, k * P:(k + 1) * P], ident[:])
                        last.then_inc(pair_full.sem, 1)
                    elif kind == "o":
                        pe.wait_ge(mT_ready.sem, mT_ready.at(l, i + 1))
                        for k in range(DK):
                            w = unit(("out", step[2], k // 4), 4)
                            last = MM(dst, mT[i % 2][:, k * P:(k + 1) * P], w[:, k % 4, :], start=k == 0, stop=k == DK - 1)
                        last.then_inc(one_full.sem, 1)
                    elif kind == "pq":
                        if i == 0:
                            pe.wait_ge(hT_ready.sem, hT_ready.at(l, 2 * NT))
                        w = unit(("pq", i // 2, 0), 16)
                        for a, b in ((0, 512), (512, NT * P)):
                            for k in range(DK):
                                last = MM(dst[:, a:b], w[:, i % 2 * 8 + k, :], hT[:, k, a:b], start=k == 0, stop=k == DK - 1)
                        last.then_inc(pair_full.sem, 1)

                def key_scores(i):
                    if i == 0:
                        pe.wait_ge(pq_ready.sem, pq_ready.at(l, 16))
                        pe.wait_ge(keys_in.sem, keys_in.at(l, 16))
                        for b in range(NB2):
                            pe.wait_ge(pair_free[b].sem, pair_free[b].at(l, pair_free[b].layer))
                    for half in range(2):
                        if i:
                            pe.wait_ge(scores_used.sem, scores_used.at(l, 2 * (i - 1) + half + 1))
                        for q in range(8):
                            last = MM(pair[half][:, q * P:(q + 1) * P], pqT[:, 8 * half + q, i * P:(i + 1) * P], keys[:, 8 * half + q, :], start=True, stop=True)
                        last.then_inc(scores_full.sem, 1)

                pe.drain().then_inc(slot_used.sem, RING)
                key_scores(0)
                for i in range(NT):
                    if i + 1 < NT:
                        key_scores(i + 1)
                    a = acc[i % 2]
                    if i >= 2:
                        pe.wait_ge(acc_used.sem, acc_used.at(l, i - 1))
                    if i == 0:
                        for b in range(NB1):
                            pe.wait_ge(one_free[b].sem, one_free[b].at(l, one_free[b].layer))
                    for c in range(2):
                        MM(a[:, c * 512:(c + 1) * 512], zeros[:], h2[:, i, c * 512:(c + 1) * 512], start=True, stop=False)
                    with pe.Fori(0, TURNS) as t:
                        for s in range(BODY):
                            pe.wait_ge(diag_ready.sem, l * diag_ready.layer + t * BODY + (i * SLOTS + s + 1))
                            for c in range(2):
                                last = MM(a[:, c * 512:(c + 1) * 512], diag[s % RING], ring[s % RING][:, D + c * 512:D + (c + 1) * 512], start=False, stop=False)
                            last.then_inc(slot_used.sem, 1)
                    for c in range(2):
                        last = MM(a[:, c * 512:(c + 1) * 512], zeros[:], h2[:, i, c * 512:(c + 1) * 512], start=False, stop=True)
                    last.then_inc(acc_full.sem, 1)
                pe.drain().then_inc(layer_end.sem, 1)
                pe.wait_ge(layer_end.sem, layer_end.at(l, 5))

        @block.scalar
        def _(act):
            A = nc.scalar.activation

            act.dma_start(ident[:], ins["ident"]).then_inc(const_in.sem, 16)
            act.dma_start(mask[:], ins["mask"]).then_inc(const_in.sem, 16)
            act.dma_start(rope[:], ins["rope"]).then_inc(const_in.sem, 16)
            act.dma_start(cond[:], ins["cond"]).then_inc(cond_in.sem, 16)
            act.wait_ge(cond_in.sem, 16)
            A(sq[:, 0:2 * DK], cond[:].rearrange("p k s -> p (k s)"), ACT.Sigmoid).then_inc(cond_ready.sem, 1)
            with act.Fori(0, L) as l:
                row = lambda name: ins[name][bass.ds(l, 1)]
                act.dma_start(gains[:], row("gains").partition_broadcast(P).rearrange("p a n -> p (a n)")).then_inc(layer_in.sem, 16)
                act.dma_start(modrow, row("b_mod").partition_broadcast(2).rearrange("p a n -> p (a n)")).then_inc(layer_in.sem, 16)
                act.dma_start(bs[:], row("b_s").rearrange("a p n -> (a p) n")).then_inc(layer_in.sem, 16)
                act.dma_start(kcT[:, :, NT * P:], row("ctx_kT").rearrange("a p g t -> (a p) g t")).then_inc(layer_in.sem, 16)
                act.dma_start(vc[:, NT:, :], row("ctx_v").rearrange("a p t n -> (a p) t n")).then_inc(layer_in.sem, 16)
                act.dma_start(grow, row("g_norm")[:, 0:D].partition_broadcast(P).rearrange("p a n -> p (a n)")).then_inc(rows_in.sem, 16)
                act.wait_ge(mod_ready.sem, mod_ready.at(l, 1))
                act.dma_start(modd, modrow).then_inc(mod_stored.sem, 16)
                act.wait_ge(mod_stored.sem, mod_stored.at(l, 16))
                for s in range(2):
                    for a, c in ((0, 1), (1, 0)):
                        act.dma_start(rows[:, s, a, :], modd[s:s + 1, c * D:(c + 1) * D].partition_broadcast(P).rearrange("p a n -> p (a n)")).then_inc(rows_in.sem, 16)

                for step in STEPS:
                    kind, i = step[0], step[1]
                    if step in ONE_NO:
                        full, j, src = one_full, ONE_NO[step], one_of(step)
                        freed = one_free[j % NB1]
                    elif step in PAIR_NO:
                        full, j, src = pair_full, PAIR_NO[step], pair_of(step)
                        freed = pair_free[j % NB2]

                    if kind == "hT":
                        phase, i = step[1:]
                        act.wait_ge(full.sem, full.at(l, j + 1))
                        A(hT[:, :, i * P:(i + 1) * P], src.rearrange("p (k t) -> p k t", k=DK), ACT.Copy).then_inc(freed.sem, 1)
                        act.drain().then_inc(hT_ready.sem, 1)
                        if step == ("hT", 0, NT - 1):
                            act.dma_start(ckvT_ctx, row("ctx_ckvT").rearrange("a p k t -> (a p) k t")).then_inc(layer_in.sem, 16)
                            act.dma_start(kr_ctx, row("ctx_kr").rearrange("a p n -> (a p) n")).then_inc(layer_in.sem, 16)
                    elif kind in ("kv", "cq", "qc"):
                        dst, ready = {"kv": (z0[i], z0_ready), "cq": (zq[i], zq_ready), "qc": (z[:, i, 512:1024], qc_in)}[kind]
                        act.wait_ge(full.sem, full.at(l, j + 1))
                        A(dst, src[:, 0:dst.shape[1]], ACT.Copy).then_inc(freed.sem, 1)
                        act.drain().then_inc(ready.sem, 1)
                        if step == ("cq", NT - 1):
                            act.wait_ge(ckv_ready.sem, ckv_ready.at(l, 1))
                            act.dma_start(outs["new_mla_ckv"][0, bass.ds(l, 1)].rearrange("a p n -> (a p) n"), z0[0][:, 0:KVL]).then_inc(latents_stored.sem, 16)
                            act.dma_start(outs["new_mla_krope"][0, bass.ds(l, 1)].rearrange("a p n -> (a p) n"), z0[0][:, KVL:288]).then_inc(latents_stored.sem, 16)
                    elif kind == "ckvT":
                        act.wait_ge(full.sem, full.at(l, j + 1))
                        A(latT[i % 2][:, 0:256], src[:, 0:256], ACT.Copy).then_inc(freed.sem, 1)
                        act.drain().then_inc(ckvT_ready.sem, 1)
                    elif kind == "ukv":
                        act.wait_ge(full.sem, full.at(l, j + 1))
                        if step[2] == 0:
                            if i >= 2:
                                act.wait_ge(pair_full.sem, pair_full.at(l, PAIR_NO[("kaT", i - 2)] + 1))
                            A(kbuf[i % 2].rearrange("p (h n) -> p h n", h=H)[:, :, 0:NOPE], src.rearrange("p (h n) -> p h n", h=H), ACT.Copy).then_inc(freed.sem, 1)
                            act.drain().then_inc(nope_in.sem, 1)
                        else:
                            A(va[:, i, :], src, ACT.Copy).then_inc(freed.sem, 1)
                    elif kind == "kaT":
                        act.wait_ge(full.sem, full.at(l, j + 1))
                        A(kaT[:, :, i * P:(i + 1) * P], src[0:AQK, :].rearrange("p (h t) -> p h t", h=H), ACT.Copy).then_inc(freed.sem, 1)
                        act.drain().then_inc(kaT_ready.sem, 1)
                    elif kind == "u":
                        act.wait_ge(full.sem, full.at(l, j + 1))
                        A(z[:, i, 0:512], src, ACT.Gelu_apprx_tanh).then_inc(freed.sem, 1)
                        act.drain().then_inc(u_in.sem, 1)
                    elif kind == "cqT":
                        act.wait_ge(full.sem, full.at(l, j + 1))
                        A(latT[i % 2], src[:, 0:QL], ACT.Copy).then_inc(freed.sem, 1)
                        act.drain().then_inc(cqT_ready.sem, 1)
                    elif kind == "uq":
                        act.wait_ge(full.sem, full.at(l, j + 1))
                        A(z[:, i, 1024 + 384 * step[2]:1024 + 384 * (step[2] + 1)], src[:, 0:384], ACT.Copy).then_inc(freed.sem, 1)
                        act.drain().then_inc(qa_in.sem, 1)
                    elif kind == "v":
                        if i == 0:
                            act.wait_ge(ka_ready.sem, ka_ready.at(l, NKT))
                            act.wait_ge(latents_stored.sem, latents_stored.at(l, 32))
                        act.wait_ge(full.sem, full.at(l, j + 1))
                        A(vb[i], src, ACT.Gelu_apprx_tanh).then_inc(freed.sem, 1)
                        act.drain().then_inc(v_in.sem, 1)
                    elif kind == "kc":
                        act.wait_ge(full.sem, full.at(l, j + 1))
                        A(kcb[i], src[:, 0:128], ACT.Copy)
                        A(vc[:, i, :], src[:, 128:256], ACT.Copy).then_inc(freed.sem, 1)
                        act.drain().then_inc(kc_in.sem, 1)
                    elif kind == "kcT":
                        act.wait_ge(full.sem, full.at(l, j + 1))
                        A(kcT[:, :, i * P:(i + 1) * P], src[0:CD, 0:256].rearrange("p (g t) -> p g t", g=CKV), ACT.Copy).then_inc(freed.sem, 1)
                        act.drain().then_inc(kcT_ready.sem, 1)
                        if i == 0:
                            act.dma_start(outs["new_swa_k"][0, bass.ds(l, 1)].rearrange("a p g n -> (a p) (g n)"), kcb[0]).then_inc(kv_stored.sem, 16)
                            act.dma_start(outs["new_swa_v"][0, bass.ds(l, 1)].rearrange("a p g n -> (a p) (g n)"), vc[:, 0, :]).then_inc(kv_stored.sem, 16)
                        if i == NT - 1:
                            act.wait_ge(kv_stored.sem, kv_stored.at(l, 32))
                    elif kind == "qT":
                        w = AQK if i % 2 == 0 else CD
                        act.wait_ge(full.sem, full.at(l, j + 1))
                        A(qTb[i % 2][0:w, :], src[0:w, :], ACT.Copy).then_inc(freed.sem, 1)
                        act.drain().then_inc(qT_ready.sem, 1)
                    elif kind == "s":
                        n = len(unit_keys(i)) * P + i % (2 * H) // H
                        act.wait_ge(max_ready.sem, max_ready.at(l, i + 1))
                        if i >= 2:
                            act.wait_ge(pair_full.sem, pair_full.at(l, PAIR_NO[("PT", i - 2)] + 1))
                        A(pb[i % 2][:, 0:n], src[:, 0:n], ACT.Exp, bias=negm[:, i:i + 1], accum_out=rsum[:, i:i + 1]).then_inc(freed.sem, 1)
                        act.drain().then_inc(exp_ready.sem, 1)
                    elif kind == "oT":
                        n = 8 if step[2] == 0 else 4
                        act.wait_ge(full.sem, full.at(l, j + 1))
                        A(oT[i][:, 8 * step[2]:8 * step[2] + n, :], src[:, 0:n * P].rearrange("p (k t) -> p k t", k=n), ACT.Copy).then_inc(freed.sem, 1)
                        act.drain().then_inc(oT_ready.sem, 1)
                        if step == ("oT", NT - 1, 1):
                            for s in range(2):
                                for dst, c in ((g1, 2), (g2, 5)):
                                    act.dma_start(dst[:, s, :], modd[s:s + 1, c * D:(c + 1) * D].partition_broadcast(P).rearrange("p a n -> p (a n)")).then_inc(gates_in.sem, 16)
                    elif kind == "g":
                        n = i * NT + step[2]
                        act.wait_ge(full.sem, full.at(l, j + 1))
                        if n >= 2:
                            act.wait_ge(merge_done.sem, merge_done.at(l, n - 1))
                        A(sg[n % 2], src, ACT.Sigmoid).then_inc(freed.sem, 1)
                        act.drain().then_inc(sg_ready.sem, 1)
                    elif kind == "mT":
                        act.wait_ge(full.sem, full.at(l, j + 1))
                        if i >= 2:
                            act.wait_ge(one_full.sem, one_full.at(l, ONE_NO[("o", i - 2, 1)] + 1))
                        A(mT[i % 2], src, ACT.Copy).then_inc(freed.sem, 1)
                        act.drain().then_inc(mT_ready.sem, 1)
                        if i == NT - 1:
                            act.dma_start(grow, row("g_norm")[:, D:2 * D].partition_broadcast(P).rearrange("p a n -> p (a n)")).then_inc(rows_in.sem, 16)
                            for s in range(2):
                                for a, c in ((0, 4), (1, 3)):
                                    act.dma_start(rows[:, s, a, :], modd[s:s + 1, c * D:(c + 1) * D].partition_broadcast(P).rearrange("p a n -> p (a n)")).then_inc(rows_in.sem, 16)
                            act.dma_start(keys, row("keysT").rearrange("a p q n -> (a p) q n")).then_inc(keys_in.sem, 16)
                    elif kind == "pq":
                        act.wait_ge(full.sem, full.at(l, j + 1))
                        A(pqT[:, i, :], src[:, 0:NT * P], ACT.Copy).then_inc(freed.sem, 1)
                        act.drain().then_inc(pq_ready.sem, 1)

                def gate_exp(i):
                    act.wait_ge(cv_ready.sem, cv_ready.at(l, i + 1))
                    A(gate[i % 2], gate[i % 2], ACT.Exp).then_inc(ce_ready.sem, 1)

                gate_exp(0)
                for i in range(NT):
                    if i + 1 < NT:
                        gate_exp(i + 1)
                    with act.Fori(0, TURNS) as t:
                        for g in range(NGRP + 1):
                            n = i * SLOTS // GRP + g
                            if g < NGRP:
                                act.wait_ge(dots_ready.sem, l * dots_ready.layer + t * NGRP + (n + 1))
                                A(gel[:, g * GRP:(g + 1) * GRP], dots[:, g * GRP:(g + 1) * GRP], ACT.Gelu_apprx_tanh).then_inc(gel_ready.sem, 1)
                            if g:
                                act.wait_ge(wts_ready.sem, l * wts_ready.layer + t * NGRP + n)
                                for s in range((g - 1) * GRP, g * GRP):
                                    act.wait_ge(slot_used.sem, l * slot_used.layer + t * BODY + (i * SLOTS + s + 1))
                                    A(diag[s % RING], ident[:], ACT.Copy, scale=wts[:, s:s + 1]).then_inc(diag_ready.sem, 1)
                act.drain().then_inc(layer_end.sem, 1)
                act.wait_ge(layer_end.sem, layer_end.at(l, 5))

        @block.vector
        def _(dve):
            V = nc.vector
            TT, TS, STT = V.tensor_tensor, V.tensor_scalar, V.scalar_tensor_tensor
            dve.wait_ge(cond_ready.sem, 1)
            cflat = cond[:].rearrange("p k s -> p (k s)")
            TT(cflat, cflat, sq[:, 0:2 * DK], ALU.mult).then_inc(cond_ready.sem, 1)
            dve.wait_ge(x_in.sem, 16 * NT)
            dve.wait_ge(const_in.sem, 16 * 3)
            dve.wait_ge(const_ready.sem, 1)

            with dve.Fori(0, L) as l:

                def gain(name, heads):
                    a, n = GAINS[name]
                    return gains[:, a:a + n].unsqueeze(1).to_broadcast([P, heads, n])

                def stat(key):
                    e, at, cols, _ = NORM_AT[key]
                    return e, ss[:, at:at + cols], rstd[:, at:at + cols]

                def squares(key, src, width):
                    e, s, _ = stat(key)
                    V.tensor_tensor_reduce(out=sq[:, 0:width], in0=src, in1=src, scale=1.0, scalar=0.0,
                                           op0=ALU.mult, op1=ALU.add, accum_out=s).then_inc(ss_ready.sem, 1)

                def head_squares(key, src3, heads, n):
                    e, s, _ = stat(key)
                    t = sq[:, 0:heads * n].rearrange("p (h n) -> p h n", h=heads)
                    TT(t, src3, src3, ALU.mult)
                    dve.drain()
                    V.tensor_reduce(s, t, AX.X, ALU.add).then_inc(ss_ready.sem, 1)

                def wait_rstd(key):
                    e, _, r = stat(key)
                    dve.wait_ge(rstd_ready.sem, rstd_ready.at(l, e + 1))
                    return r

                def head_norm(key, src3, heads, n, gname):
                    r = wait_rstd(key)
                    TT(src3, src3, r.unsqueeze(2).to_broadcast([P, heads, n]), ALU.mult)
                    dve.drain()
                    TT(src3, src3, gain(gname, heads), ALU.mult)
                    dve.drain()

                def rotate(src3, heads, half, tile, at):
                    c = rope[:, tile - 1, at:at + half].unsqueeze(1).to_broadcast([P, heads, half])
                    s = rope[:, tile - 1, at + half:at + 2 * half].unsqueeze(1).to_broadcast([P, heads, half])
                    a, b = src3[:, :, 0:half], src3[:, :, half:2 * half]
                    t = sq[:, 0:2 * heads * half].rearrange("p (e h n) -> p e h n", e=2, h=heads)
                    TT(t[:, 0], a, s, ALU.mult)
                    TT(t[:, 1], b, s, ALU.mult)
                    dve.drain()
                    TT(a, a, c, ALU.mult)
                    TT(b, b, c, ALU.mult)
                    dve.drain()
                    TT(a, a, t[:, 1], ALU.subtract)
                    TT(b, b, t[:, 0], ALU.add)
                    dve.drain()

                def model_norm(phase):
                    _, s, _ = stat(("n", phase))
                    for i in range(NT):
                        last = V.tensor_tensor_reduce(out=sq[:], in0=x[:, i, :], in1=x[:, i, :], scale=1.0, scalar=0.0,
                                                      op0=ALU.mult, op1=ALU.add, accum_out=s[:, i:i + 1])
                        if i < NT - 1:
                            dve.drain()
                    last.then_inc(ss_ready.sem, 1)
                    dve.wait_ge(rows_in.sem, rows_in.at(l, 80 * (phase + 1)))
                    for st in range(2):
                        STT(rows[:, st, 0, :], rows[:, st, 0, :], 1.0, grow, ALU.add, ALU.mult)
                    dve.drain()
                    r = wait_rstd(("n", phase))
                    for i in range(NT):
                        st = min(i, 1)
                        if phase == 0 and i >= 2:
                            dve.wait_ge(pair_full.sem, pair_full.at(l, PAIR_NO[("hT", 0, i - 2)] + 1))
                        dst = h2[:, i, :] if phase else hbuf[i % 2]
                        STT(dst, x[:, i, :], r[:, i:i + 1], rows[:, st, 0, :], ALU.mult, ALU.mult)
                        dve.drain()
                        TT(dst, dst, rows[:, st, 1, :], ALU.add).then_inc(h_ready.sem, 1)

                dve.wait_ge(layer_in.sem, layer_in.at(l, 80))
                for name, d in (("qa", AQK), ("qc", CD)):
                    a, n = GAINS[name]
                    TS(gains[:, a:a + n], gains[:, a:a + n], float(d) ** -0.5, None, ALU.mult)
                for b in range(12):
                    j = ONE_NO[("mod", b)]
                    dve.wait_ge(one_full.sem, one_full.at(l, j + 1))
                    last = TT(modrow[:, b * 512:(b + 1) * 512], one_of(("mod", b))[0:2, :], modrow[:, b * 512:(b + 1) * 512], ALU.add)
                    last.then_inc(one_free[j % NB1].sem, 1)
                dve.drain().then_inc(mod_ready.sem, 1)

                model_norm(0)

                for i in range(NT):
                    dve.wait_ge(z0_ready.sem, z0_ready.at(l, i + 1))
                    squares(("ckv", i), z0[i][:, 0:KVL], KVL)
                    dve.drain()
                a, n = GAINS["kv"]
                for i in range(NT):
                    r = wait_rstd(("ckv", i))
                    STT(z0[i][:, 0:KVL], z0[i][:, 0:KVL], r, gains[:, a:a + n], ALU.mult, ALU.mult).then_inc(ckv_ready.sem, 1)
                for i in range(NT):
                    dve.wait_ge(zq_ready.sem, zq_ready.at(l, i + 1))
                    squares(("cq", i), zq[i], QL)
                    dve.drain()
                a, n = GAINS["q"]
                for i in range(NT):
                    r = wait_rstd(("cq", i))
                    STT(zq[i], zq[i], r, gains[:, a:a + n], ALU.mult, ALU.mult).then_inc(cq_ready.sem, 1)

                for i in range(NKT):
                    k3 = kbuf[i % 2].rearrange("p (h n) -> p h n", h=H)
                    if i < NT:
                        kr = z0[i][:, KVL:288]
                    else:
                        if i == NT:
                            dve.wait_ge(layer_in.sem, layer_in.at(l, layer_in.layer))
                        kr = kr_ctx[:, (i - NT) * ROPE:(i - NT + 1) * ROPE]
                    dve.wait_ge(nope_in.sem, nope_in.at(l, i + 1))
                    V.tensor_copy(k3[:, :, NOPE:], kr.unsqueeze(1).to_broadcast([P, H, ROPE]))
                    dve.drain()
                    head_squares(("ka", i), k3, H, AQK)
                    head_norm(("ka", i), k3, H, AQK, "ka")
                    if 1 <= i < NT:
                        rotate(k3[:, :, NOPE:], H, ROPE // 2, i, 0)
                    dve.drain().then_inc(ka_ready.sem, 1)

                for i in range(NT):
                    q3 = z[:, i, 1024:1792].rearrange("p (h n) -> p h n", h=H)
                    dve.wait_ge(qa_in.sem, qa_in.at(l, 2 * i + 2))
                    head_squares(("qa", i), q3, H, AQK)
                    dve.drain()

                for i in range(NT):
                    dve.wait_ge(v_in.sem, v_in.at(l, i + 1))
                    squares(("v", i), vb[i], 512)
                    dve.drain()
                for i in range(NT):
                    r = wait_rstd(("v", i))
                    a, n = GAINS["v"]
                    STT(vb[i], vb[i], r, gains[:, a:a + n], ALU.mult, ALU.mult).then_inc(v_ready.sem, 1)
                for i in range(NT):
                    q3 = z[:, i, 1024:1792].rearrange("p (h n) -> p h n", h=H)
                    head_norm(("qa", i), q3, H, AQK, "qa")
                    if i:
                        rotate(q3[:, :, NOPE:], H, ROPE // 2, i, 0)
                    dve.drain().then_inc(qa_ready.sem, 1)
                for i in range(NT):
                    j = ONE_NO[("vm", i)]
                    dve.wait_ge(u_in.sem, u_in.at(l, i + 1))
                    dve.wait_ge(one_full.sem, one_full.at(l, j + 1))
                    t = sq[:, 0:512].rearrange("p (g n) -> p g n", g=H)
                    TT(t, one_of(("vm", i)).rearrange("p (g n) -> p g n", g=H), bs[:].unsqueeze(2).to_broadcast([P, H, 64]), ALU.add).then_inc(one_free[j % NB1].sem, 1)
                    dve.drain()
                    TT(z[:, i, 0:512], z[:, i, 0:512], sq[:, 0:512], ALU.mult).then_inc(ob_ready.sem, 1)
                    dve.drain()

                for i in range(NT):
                    q3 = z[:, i, 512:1024].rearrange("p (h n) -> p h n", h=H)
                    dve.wait_ge(qc_in.sem, qc_in.at(l, i + 1))
                    head_squares(("qc", i), q3, H, CD)
                    dve.drain()
                for i in range(NT):
                    k3 = kcb[i].rearrange("p (h n) -> p h n", h=CKV)
                    dve.wait_ge(kc_in.sem, kc_in.at(l, i + 1))
                    head_squares(("kc", i), k3, CKV, CD)
                    dve.drain()
                for i in range(NT):
                    k3 = kcb[i].rearrange("p (h n) -> p h n", h=CKV)
                    head_norm(("kc", i), k3, CKV, CD, "kc")
                    if i:
                        rotate(k3, CKV, CD // 2, i, 32)
                    dve.drain().then_inc(kc_ready.sem, 1)
                for i in range(NT):
                    q3 = z[:, i, 512:1024].rearrange("p (h n) -> p h n", h=H)
                    head_norm(("qc", i), q3, H, CD, "qc")
                    if i:
                        rotate(q3, H, CD // 2, i, 32)
                    dve.drain().then_inc(qc_ready.sem, 1)

                for step in STEPS:
                    kind, i = step[0], step[1]
                    if kind == "s":
                        n = len(unit_keys(i)) * P + i % (2 * H) // H
                        dve.wait_ge(pair_full.sem, pair_full.at(l, PAIR_NO[step] + 1))
                        V.tensor_reduce(negm[:, i:i + 1], pair_of(step)[:, 0:n], AX.X, ALU.max, negate=True).then_inc(max_ready.sem, 1)
                    elif kind == "PT":
                        n = len(unit_keys(i)) * P
                        j = PAIR_NO[step]
                        dve.wait_ge(pair_full.sem, pair_full.at(l, j + 1))
                        if i >= 2:
                            dve.wait_ge(o_done.sem, o_done.at(l, i - 1))
                        V.tensor_copy(ptb[i % 2][:, 0:n], pair_of(step)[:, 0:n]).then_inc(pair_free[j % NB2].sem, 1)
                        dve.drain().then_inc(pt_ready.sem, 1)
                    elif kind == "O" and i % H == H - 1:
                        t, m = divmod(i // H, 2)
                        r = rsum[:, i - H + 1:i + 1]
                        dve.wait_ge(o_done.sem, o_done.at(l, i + 1))
                        V.reciprocal(r, r)
                        dve.drain()
                        if m == 0 and t:
                            dve.wait_ge(pair_full.sem, pair_full.at(l, PAIR_NO[("oT", t - 1, 1)] + 1))
                        TT(otok[:, 512 * m:512 * (m + 1)].rearrange("p (h n) -> p h n", h=H),
                           one[m].rearrange("p (h n) -> p h n", h=H), r.unsqueeze(2).to_broadcast([P, H, 64]), ALU.mult).then_inc(o_moved.sem, 1)
                    elif kind == "p":
                        bc, t = step[1:]
                        b, c = divmod(bc, 2)
                        n = bc * NT + t
                        j = ONE_NO[step]
                        dve.wait_ge(sg_ready.sem, sg_ready.at(l, n + 1))
                        dve.wait_ge(one_full.sem, one_full.at(l, j + 1))
                        m = merged[:, t, c * 512:(c + 1) * 512]
                        if b == 0:
                            TT(m, one_of(step), sg[n % 2], ALU.mult).then_inc(one_free[j % NB1].sem, 1)
                            dve.drain().then_inc(merge_done.sem, 1)
                        else:
                            TT(sq[:, 0:512], one_of(step), sg[n % 2], ALU.mult).then_inc(one_free[j % NB1].sem, 1)
                            dve.drain()
                            TT(m, m, sq[:, 0:512], ALU.add).then_inc(merge_done.sem, 1)
                            dve.drain()
                    elif kind == "o":
                        c = step[2]
                        j = ONE_NO[step]
                        if i == 0 and c == 0:
                            dve.wait_ge(gates_in.sem, gates_in.at(l, 64))
                        dve.wait_ge(one_full.sem, one_full.at(l, j + 1))
                        TT(sq[:, 0:512], one_of(step), g1[:, min(i, 1), c * 512:(c + 1) * 512], ALU.mult).then_inc(one_free[j % NB1].sem, 1)
                        dve.drain()
                        xs = x[:, i, c * 512:(c + 1) * 512]
                        TT(xs, xs, sq[:, 0:512], ALU.add)
                        dve.drain()

                model_norm(1)
                V.memset(iota, 0.0)
                dve.drain()
                for w in (1, 2, 4, 8):
                    TS(iota[:, w:2 * w], iota[:, 0:w], float(w), None, ALU.add)
                    dve.drain()

                def top16(vals, inds, src, tmp):
                    V.max(vals[:, 0:8], src)
                    dve.drain()
                    V.max_index(inds[:, 0:8], vals[:, 0:8], src)
                    V.match_replace(tmp, vals[:, 0:8], src, LOW)
                    dve.drain()
                    V.max(vals[:, 8:16], tmp)
                    dve.drain()
                    V.max_index(inds[:, 8:16], vals[:, 8:16], tmp)

                def choose_experts(i):
                    for half in range(2):
                        dve.wait_ge(scores_full.sem, scores_full.at(l, 2 * i + half + 1))
                        alone(dve)
                        for q in range(8):
                            n = half * 8 + q
                            top16(v16[:, n * 16:(n + 1) * 16], i16[:, n * 16:(n + 1) * 16],
                                  pair[half][:, q * P:(q + 1) * P], tmpk[q % 2][:, 0:P])
                        dve.drain().then_inc(scores_used.sem, 1)
                    vv = v16.rearrange("p (h e k) -> p h e k", h=H, e=2)
                    c4 = cand.rearrange("p (h a b) -> p h a b", h=H, a=16)
                    TT(c4, vv[:, :, 0, :].unsqueeze(3).to_broadcast([P, H, 16, 16]),
                       vv[:, :, 1, :].unsqueeze(2).to_broadcast([P, H, 16, 16]), ALU.add)
                    V.tensor_copy(i16f, i16)
                    dve.drain()
                    for h in range(H):
                        top16(cv[:, h * 16:(h + 1) * 16], ci[:, h * 16:(h + 1) * 16], cand[:, h * 256:(h + 1) * 256], tmpk[h % 2])
                    dve.drain()
                    g3 = gate[i % 2].rearrange("p (h k) -> p h k", h=H)
                    cv3 = cv.rearrange("p (h k) -> p h k", h=H)
                    TT(g3, cv3, cv3[:, :, 0:1].to_broadcast([P, H, 16]), ALU.subtract)
                    TS(cab[:, 0:128], ci, 4, None, ALU.logical_shift_right)
                    TS(cab[:, 128:256], ci, 15, None, ALU.bitwise_and)
                    dve.drain().then_inc(cv_ready.sem, 1)
                    V.tensor_copy(cabf, cab)
                    dve.drain()
                    fi = i16f.rearrange("p (h e k) -> p h e k", h=H, e=2)
                    for e in range(2):
                        pos = cabf[:, e * 128:(e + 1) * 128].rearrange("p (h k) -> p h k", h=H)
                        TT(c4, pos.unsqueeze(3).to_broadcast([P, H, 16, 16]),
                           iota.unsqueeze(1).unsqueeze(1).to_broadcast([P, H, 16, 16]), ALU.is_equal)
                        dve.drain()
                        TT(c4, c4, fi[:, :, e, :].unsqueeze(2).to_broadcast([P, H, 16, 16]), ALU.mult)
                        dve.drain()
                        V.tensor_reduce(sel[:, e * 128:(e + 1) * 128], cand.rearrange("p (n a) -> p n a", a=16), AX.X, ALU.add)
                        dve.drain()
                    STT(sel[:, 0:128], sel[:, 0:128], 128.0, sel[:, 128:256], ALU.mult, ALU.add)
                    dve.drain()
                    TS(idx[i % 2], sel[:, 0:128], base[:], None, ALU.add)
                    dve.wait_ge(ce_ready.sem, ce_ready.at(l, i + 1))
                    V.tensor_reduce(esum, g3, AX.X, ALU.add)
                    dve.drain()
                    V.reciprocal(esum, esum)
                    dve.drain()
                    TT(g3, g3, esum.unsqueeze(2).to_broadcast([P, H, 16]), ALU.mult)
                    dve.drain()

                dve.wait_ge(pq_ready.sem, pq_ready.at(l, 16))
                choose_experts(0)
                for i in range(NT):
                    if i + 1 < NT:
                        choose_experts(i + 1)
                    with dve.Fori(0, TURNS) as t:
                        dve.drain()
                        V.tensor_copy(ihead, idx[i % 2][:, bass.ds(t * BODY, BODY)])
                        V.tensor_copy(ghead, gate[i % 2][:, bass.ds(t * BODY, BODY)])
                        dve.drain().then_inc(head_ready.sem, 1)
                        for g in range(NGRP + 1):
                            n = i * SLOTS // GRP + g
                            if g < NGRP:
                                for s in range(g * GRP, (g + 1) * GRP):
                                    r = s % RING
                                    dve.wait_ge(g_land[r].sem, l * g_land[r].layer + t * (16 * BODY // RING) + 16 * (i * SLOTS // RING + s // RING + 1))
                                    last = V.tensor_tensor_reduce(out=sq[:], in0=ring[r][:, 0:D], in1=h2[:, i, :], scale=1.0, scalar=0.0,
                                                                  op0=ALU.mult, op1=ALU.add, accum_out=dots[:, s:s + 1])
                                    if s % GRP < GRP - 1:
                                        dve.drain()
                                last.then_inc(dots_ready.sem, 1)
                                dve.drain()
                            if g:
                                dve.wait_ge(gel_ready.sem, l * gel_ready.layer + t * NGRP + n)
                                a, b = (g - 1) * GRP, g * GRP
                                TT(wts[:, a:b], gel[:, a:b], ghead[:, a:b], ALU.mult).then_inc(wts_ready.sem, 1)
                    dve.wait_ge(acc_full.sem, acc_full.at(l, i + 1))
                    TT(sq[:], acc[i % 2], g2[:, min(i, 1), :], ALU.mult).then_inc(acc_used.sem, 1)
                    dve.drain()
                    TT(x[:, i, :], x[:, i, :], sq[:], ALU.add)
                    dve.drain()
                TS(base[:], base[:], float(NEXP), None, ALU.add)
                dve.drain().then_inc(layer_end.sem, 1)
                dve.wait_ge(layer_end.sem, layer_end.at(l, 5))


def lay_out(inputs):
    import numpy as np

    a = {k: np.ascontiguousarray(v) for k, v in inputs.items()}

    def unit(l, name):
        kind, b, k = name
        blocks = lambda w: w.reshape(-1, P, w.shape[1]).transpose(1, 0, 2)
        w_in = a["w_in"][l]
        first = {"cq": (0, 384), "kv": (384, 672), "u": (672, 1184), "v": (1184, 1696), "qc": (1696, 2208), "kc": (2208, 2464)}
        if kind in first:
            lo, hi = first[kind]
            return blocks(w_in[512 * k:512 * (k + 1), lo:hi])
        if kind == "mod":
            return blocks(a["w_mod"][l][512 * k:512 * (k + 1), 512 * b:512 * (b + 1)])
        if kind == "gate":
            return blocks(w_in[512 * k:512 * (k + 1), 2464 + 512 * b:2464 + 512 * (b + 1)])
        if kind == "proj":
            w = a[("w_o_a", "w_o_b", "w_o_c")[b // 2]][l]
            return blocks(w[:, 512 * (b % 2):512 * (b % 2 + 1)])
        if kind == "out":
            return blocks(a["w_out"][l][512 * k:512 * (k + 1), 512 * b:512 * (b + 1)])
        if kind == "ukv":
            w = a["w_ukv"][l].reshape(KVL, H, 2, 64).transpose(0, 2, 1, 3).reshape(KVL, D)
            return blocks(w)
        if kind == "uq":
            return blocks(a["w_uq"][l][:, 384 * k:384 * (k + 1)])
        if kind == "ws":
            return a["w_s_b"][l].transpose(2, 0, 1)
        if kind == "pq":
            w = a["w_pq"][l][:, 256 * b:256 * (b + 1)].reshape(DK, P, 2, P)
            return w.transpose(1, 2, 0, 3)

    r = {"x_prompt": a["x_prompt"], "x_sample": a["x_sample"]}
    weights = np.empty((L, WTOTAL), np.float32)
    for l in range(L):
        for name, (_, at, size) in UNO.items():
            weights[l, at:at + P * size] = unit(l, name).reshape(-1)
    r["weights"] = weights
    r["experts"] = np.concatenate([a["peer_u"], a["peer_v"]], axis=2).reshape(L * NEXP, 2 * D)
    r["gains"] = np.concatenate([a[n] for n in ("g_kv_lora", "g_q_lora", "g_qk_a_q", "g_qk_a_k", "g_v_b", "g_qk_c_q", "g_qk_c_k", "sink_c")], axis=1)
    r["b_mod"] = a["b_mod"]
    r["g_norm"] = np.concatenate([a["g_attn_norm"], a["g_ffn_norm"]], axis=1)
    r["b_s"] = np.ascontiguousarray(a["b_s_b"].transpose(0, 2, 1))
    r["ctx_kT"] = np.ascontiguousarray(a["cache_swa_k"][0].transpose(0, 3, 2, 1))
    r["ctx_v"] = np.ascontiguousarray(a["cache_swa_v"][0].reshape(L, 2, P, CKV * CD).transpose(0, 2, 1, 3))
    r["ctx_ckvT"] = np.ascontiguousarray(a["cache_mla_ckv"][0].reshape(L, 2 * P, 2, P).transpose(0, 3, 2, 1))
    r["ctx_kr"] = np.ascontiguousarray(a["cache_mla_krope"][0].reshape(L, 2, P, ROPE).transpose(0, 2, 1, 3).reshape(L, P, 2 * ROPE))
    r["keysT"] = np.ascontiguousarray(a["peer_keys"].reshape(L, 16, P, P).transpose(0, 3, 1, 2))
    cond = np.concatenate([a["c_ctx"][None], a["c"]], axis=0)
    r["cond"] = np.ascontiguousarray(cond.reshape(2, DK, P).transpose(2, 1, 0))
    r.update(shape_constants())
    return r


def shape_constants():
    import numpy as np

    q, k = np.arange(P)[:, None], np.arange(P)[None, :]
    mask = np.stack([np.where(k >= q, 0.0, NEG), np.where(k <= q, 0.0, NEG)], axis=1).astype(np.float32)
    pos = np.arange(4 * P)
    row, col = (pos // 64).astype(np.float32), (pos % 64).astype(np.float32)
    parts = []
    for dim in (ROPE, CD):
        quarter = dim // 4
        inv = (np.float32(10000.0) ** (-np.arange(quarter, dtype=np.float32) / np.float32(quarter))).astype(np.float32)
        ang = np.concatenate([row[:, None] * inv, col[:, None] * inv], axis=-1)
        parts += [np.cos(ang), np.sin(ang)]
    rope = np.concatenate(parts, axis=1).astype(np.float32).reshape(4, P, 96).transpose(1, 0, 2)
    return {"ident": np.eye(P, dtype=np.float32), "mask": mask, "rope": np.ascontiguousarray(rope)}


_OUTS = {
    "y_prompt": (1, 128, 1024), "y_sample": (1, 512, 1024), "new_mla_ckv": (1, 2, 128, 256),
    "new_mla_krope": (1, 2, 128, 32), "new_swa_k": (1, 2, 128, 2, 64), "new_swa_v": (1, 2, 128, 2, 64),
}


def kernel(**inputs):
    import concourse.bacc as _bacc
    from concourse.bass_utils import run_bass_kernel_spmd as _run

    nc = _bacc.Bacc("TRN2", target_bir_lowering=False, num_devices=1)
    arrays = lay_out(inputs)
    ins = {n: nc.dram_tensor(f"in_{n}", v.shape, mybir.dt.from_np(v.dtype), kind="ExternalInput").ap() for n, v in arrays.items()}
    outs = {n: nc.dram_tensor(f"out_{n}", s, F32, kind="ExternalOutput").ap() for n, s in _OUTS.items()}
    build(nc, ins, outs)
    r = _run(nc, [{f"in_{n}": v for n, v in arrays.items()}], core_ids=[0])
    return tuple(r.results[0][f"out_{n}"] for n in _OUTS)
```

```python
from contextlib import ExitStack

import concourse.bass as bass
from concourse import mybir

ALU = mybir.AluOpType
ACT = mybir.ActivationFunctionType
AX = mybir.AxisListType
F32 = mybir.dt.float32
U32 = mybir.dt.uint32

P = 128
D = 1024
L = 2
NT = 5
NKT = NT + 2
DK = D // P
EPS = 1e-6
H = 8
NOPE, ROPE, AQK = 64, 32, 96
QL, KVL = 384, 256
CD, CKV = 64, 2
TOPK = 16
NEXP = 128 * 128
SLOTS = H * TOPK
NEG = -1e30
LOW = -3.0e38

GAINS = {}
_at = 0
for _n, _s in (("kv", KVL), ("q", QL), ("qa", AQK), ("ka", AQK), ("v", 512), ("qc", CD), ("kc", CD), ("sink", H)):
    GAINS[_n] = (_at, _s)
    _at += _s
NG = _at

UNIT = 2048
NU = 5
UNITS = ([(("mod", b, k), 2048) for b in range(12) for k in range(2)]
         + [(("kv", 0, k), 4 * 288) for k in range(2)]
         + [(("cq", 0, k), 4 * 384) for k in range(2)]
         + [(("ukv", 0, 0), 2048)]
         + [(("u", 0, k), 2048) for k in range(2)]
         + [(("uq", 0, k), 3 * 384) for k in range(2)]
         + [(("v", 0, k), 2048) for k in range(2)]
         + [(("kc", 0, k), 1024) for k in range(2)]
         + [(("ws", 0, 0), 1024)]
         + [(("qc", 0, k), 2048) for k in range(2)]
         + [((n, 2 * b + c, k), 2048) for b in range(3) for c in range(2) for n, k in (("gate", 0), ("gate", 1), ("proj", 0))]
         + [(("out", c, k), 2048) for c in range(2) for k in range(2)]
         + [(("pq", q, 0), 2048) for q in range(8)])
UNO = {}
_at = 0
for _i, (_n, _s) in enumerate(UNITS):
    UNO[_n] = (_i, _at, _s)
    _at += P * _s
WTOTAL = _at


HEAD = 12 - NT


def tensor_steps():
    s = []
    for b in range(12):
        s += [("mod", b)]
        s += [("hT", 0, b - HEAD)] if b >= HEAD else []
    s += [("kv", i) for i in range(NT)] + [("cq", i) for i in range(NT)]
    s += [("ckvT", 0)]
    for i in range(NKT):
        s += [("ukv", i, 0), ("ukv", i, 1)]
        s += [("ckvT", i + 1)] if i + 1 < NT else [("cqT", i + 1 - NT)]
        s += [("kaT", i - 1)] if i else []
        s += [("u", i)] if i < NT else [("uq", i - NT, 0), ("uq", i - NT, 1)]
    s += [("kaT", NKT - 1)]
    for i in range(NKT - NT, NT):
        s += [("cqT", i + 1)] if i + 1 < NT else []
        s += [("uq", i, 0), ("uq", i, 1)]
    s += [("v", i) for i in range(NT)] + [("kc", i) for i in range(NT)]
    s += [("vm", i) for i in range(NT)]
    for i in range(NT):
        s += [("qc", i)] + {2: [("kcT", 0), ("kcT", 1)], 3: [("kcT", 2), ("kcT", 3), ("kcT", 4)]}.get(i, [])
    n = 2 * H * NT
    s += [("qT", 0)]
    for u in range(n + 2):
        if u < n:
            s += [("s", u)]
        if 1 <= u <= n:
            s += [("PT", u - 1)]
        if u % H == 5 and u + 3 < n:
            s += [("qT", u // H + 1)]
        if u >= 2:
            s += [("O", u - 2)]
            if u - 2 > 2 * H and (u - 2) % (2 * H) == 1:
                s += [("oT", (u - 2) // (2 * H) - 1, j) for j in range(2)]
    s += [("oT", NT - 1, j) for j in range(2)]
    for bc in range(6):
        for i in range(NT):
            s += [("g", bc, i), ("p", bc, i)]
    s += [("mT", 0)]
    for i in range(NT):
        s += [("o", i, 0)] + ([("mT", i + 1)] if i + 1 < NT else []) + [("o", i, 1)]
        s += [("hT", 1, i - 1)] if i else []
    s += [("hT", 1, NT - 1)]
    for q in range(16):
        s += [("pq", q)]
        s += [("sc", q - 1)] if q else []
    s += [("sc", 15)]
    return s


STEPS = tensor_steps()
ONE = ("mod", "kv", "cq", "ukv", "u", "uq", "v", "vm", "qc", "kc", "g", "p", "o")
TWO = ("hT", "ckvT", "kaT", "cqT", "kcT", "qT", "s", "PT", "oT", "mT", "pq", "sc")
ONES = [s for s in STEPS if s[0] in ONE]
PAIRS = [s for s in STEPS if s[0] in TWO]
ONE_NO = {s: j for j, s in enumerate(ONES)}
PAIR_NO = {s: j for j, s in enumerate(PAIRS)}
NB1, NB2 = 2, 3

LAST_USE = {}
for _n in UNO:
    LAST_USE[_n] = {"mod": lambda b: ("mod", b), "kv": lambda b: ("kv", 4), "cq": lambda b: ("cq", 4),
                    "ukv": lambda b: ("ukv", NKT - 1, 1), "u": lambda b: ("u", 4), "uq": lambda b: ("uq", 4, 1),
                    "v": lambda b: ("v", 4), "ws": lambda b: ("vm", 4), "qc": lambda b: ("qc", 4),
                    "kc": lambda b: ("kc", 4), "gate": lambda b: ("p", b, 4), "proj": lambda b: ("p", b, 4),
                    "out": lambda b: ("o", 4, 1), "pq": lambda b: ("pq", 2 * b + 1)}[_n[0]](_n[1])

NORMS = ([(("n", 0), NT, D)] + [(("ckv", i), 1, KVL) for i in range(NT)] + [(("cq", i), 1, QL) for i in range(NT)]
         + [(("ka", i), H, AQK) for i in range(NKT)] + [(("qa", i), H, AQK) for i in range(NT)]
         + [(("v", i), 1, 512) for i in range(NT)]
         + [(("kc", i), CKV, CD) for i in range(NT)] + [(("qc", i), H, CD) for i in range(NT)]
         + [(("n", 1, i), 1, D) for i in range(NT)])
NORM_AT = {}
_at = 0
for _i, (_k, _c, _w) in enumerate(NORMS):
    NORM_AT[_k] = (_i, _at, _c, _w)
    _at += _c
NSTAT = _at


def a_keys(i):
    return [0] if i == 0 else list(range(1, NKT))


def c_keys(i):
    return [0] if i == 0 else [NT, NT + 1] + [t for t in (i - 1, i, i + 1) if 1 <= t < NT]


def unit_keys(u):
    i, r = divmod(u, 2 * H)
    return a_keys(i) if r < H else c_keys(i)


RING = 8
GRP = 2
BODY = 32
TURNS = SLOTS // BODY
NGRP = BODY // GRP
HALF = BODY // 2
REFILL = NGRP // 2 + 1


class Signal:

    def __init__(self, sem, layer):
        self.sem, self.layer = sem, layer

    def at(self, l, n):
        return l * self.layer + n


def build(nc, ins, outs):
    with ExitStack() as ctx:
        sb = lambda n, s, d=F32: ctx.enter_context(nc.sbuf_tensor(n, s, d))

        def signal(name, layer):
            return Signal(ctx.enter_context(nc.semaphore(name)), layer)

        x = sb("x", [P, NT, D])
        z = sb("z", [P, NT, 1792])
        kcv = sb("kcv", [P, 2688])
        big = sb("big", [P, 7168 + 3584])
        arena = sb("arena", [P, NU * UNIT + NT * D + 6240])
        sq = sb("sq", [P, D])
        ident = sb("ident", [P, P])
        zeros = sb("zeros", [P, P])
        ones = sb("ones", [1, P])
        mask = sb("mask", [P, 2, P])
        rope = sb("rope", [P, 4, 96])
        gains = sb("gains", [P, NG])
        bs = sb("bs", [P, H])
        cond = sb("cond", [P, DK, 2])
        ss = sb("ss", [P, NSTAT])
        rstd = sb("rstd", [P, NSTAT])
        negm = sb("negm", [P, 2 * H * NT])
        rsum = sb("rsum", [P, 2 * H * NT])
        base = sb("base", [P, 1])
        mhalf = sb("mhalf", [P, 1])

        wring = [arena[:, r * UNIT:(r + 1) * UNIT] for r in range(NU)]
        hT = arena[:, NU * UNIT:NU * UNIT + NT * D].rearrange("p (k t) -> p k t", k=DK)
        S0 = NU * UNIT + NT * D
        scr = lambda a, n: arena[:, S0 + a:S0 + a + n]
        hbuf = [scr(0, D), scr(D, D)]
        z0 = [scr(288 * i, 288) for i in range(NT)]
        kr_ctx = scr(1440, 64)
        ckvT_ctx = scr(1504, 512).rearrange("p (k t) -> p k t", k=2)
        zq = [scr(2016 + QL * i, QL) for i in range(NT)]
        kbuf = [scr(3936 + 768 * r, 768) for r in range(2)]
        latT = [scr(5472 + QL * r, QL) for r in range(2)]
        vb = [scr(512 * i, 512) for i in range(NT)]
        kcb = [scr(2560 + 128 * i, 128) for i in range(NT)]
        otok = scr(0, D)
        pb = [scr(1024 + 776 * r, 776) for r in range(2)]
        ptb = [scr(2576 + 768 * r, 768) for r in range(2)]
        qTb = [scr(4112, D), scr(5136, D)]
        sg = [scr(512 * r, 512) for r in range(2)]
        mT = [scr(1024 + D * r, D) for r in range(2)]

        kaT = big[0:AQK, 0:7168].rearrange("p (h t) -> p h t", h=H)
        va = big[:, 7168:].rearrange("p (t n) -> p t n", t=NKT)
        merged = big[:, 0:NT * D].rearrange("p (t n) -> p t n", t=NT)
        g1 = big[:, 5120:7168].rearrange("p (s n) -> p s n", s=2)
        rows = big[:, 0:4096].rearrange("p (s a n) -> p s a n", s=2, a=2)
        grow = big[:, 4096:5120]
        scale2 = big[:, 7168:9216].rearrange("p (s n) -> p s n", s=2)
        grow2 = big[:, 9216:10240]
        shift2 = scr(3072, 2 * D).rearrange("p (s n) -> p s n", s=2)
        pqT = big[:, 0:16 * NT * P].rearrange("p (t q n) -> p t q n", t=NT, q=16)
        kcT = kcv[0:CD, 0:1792].rearrange("p (g t) -> p g t", g=CKV)
        vc = kcv[:, 1792:2688].rearrange("p (t n) -> p t n", t=NKT)
        g2 = kcv[:, 0:2048].rearrange("p (s n) -> p s n", s=2)
        modrow = z[0:2, :, :].rearrange("p t n -> p (t n)")[:, 0:6144]
        zflat = z[:, :, :].rearrange("p t n -> p (t n)")
        h2 = zflat[:, 0:NT * D].rearrange("p (t n) -> p t n", t=NT)
        keys = zflat[:, 5120:7168].rearrange("p (q n) -> p q n", q=16)
        oT = [z[:, i, 0:1536].rearrange("p (k t) -> p k t", k=12) for i in range(NT)]

        ring = [arena[:, r * 2 * D:(r + 1) * 2 * D] for r in range(RING)]
        T0 = RING * 2 * D - S0
        cand = scr(T0, 512)
        sc4 = scr(T0 + 512, 512)
        v16 = scr(T0 + 1024, 64)
        i16 = scr(T0 + 1088, 64).bitcast(U32)
        i16f = scr(T0 + 1152, 64)
        tmpk = [scr(T0 + 1216 + 256 * r, 256) for r in range(2)]
        cv = scr(T0 + 1728, BODY)
        ci = scr(T0 + 1760, BODY).bitcast(U32)
        cab = scr(T0 + 1792, 2 * BODY).bitcast(U32)
        cabf = scr(T0 + 1856, 2 * BODY)
        sel = scr(T0 + 1920, 2 * BODY)
        esum = scr(T0 + 1984, 2)
        iota = scr(T0 + 1992, 16)
        inext = scr(T0 + 2016, BODY).bitcast(U32)
        gnext = scr(T0 + 2048, BODY)
        ihead = scr(T0 + 2080, BODY).bitcast(U32)
        ghead = scr(T0 + 2112, BODY)
        dots = scr(T0 + 2144, BODY)
        gel = scr(T0 + 2176, BODY)
        wts = scr(T0 + 2208, BODY)
        diag = [scr(T0 + 2240 + P * r, P) for r in range(RING)]
        assert T0 + 2240 + RING * P <= 6240

        ps = ctx.enter_context(nc.psum_tensor("ps", [P, 8, 512], F32))
        one = [ps[:, b, :] for b in range(NB1)]
        pair = [ps[:, 2 + 2 * b:4 + 2 * b, :].rearrange("p a n -> p (a n)") for b in range(NB2)]
        acc = [ps[:, 0:2, :].rearrange("p a n -> p (a n)"), pair[2]]
        modd = nc.dram_tensor("mod_rows", [2, 6144], F32, kind="Internal").ap()

        def uses(n, total, b):
            return (total - b + n - 1) // n

        x_in = signal("x_in", 0)
        const_in = signal("const_in", 0)
        cond_in = signal("cond_in", 0)
        cond_ready = signal("cond_ready", 0)
        const_ready = signal("const_ready", 0)
        layer_end = signal("layer_end", 5)
        layer_in = signal("layer_in", 16 * 7)
        w_land = [signal(f"w_land{r}", 16 * uses(NU, len(UNITS), r)) for r in range(NU)]
        one_full = signal("one_full", len(ONES))
        one_free = [signal(f"one_free{b}", uses(NB1, len(ONES), b)) for b in range(NB1)]
        pair_full = signal("pair_full", len(PAIRS))
        pair_free = [signal(f"pair_free{b}", uses(NB2, len(PAIRS), b)) for b in range(NB2)]
        mod_stored = signal("mod_stored", 32)
        mod_ready = signal("mod_ready", 2)
        rows_in = signal("rows_in", 2 * 16 * 5)
        gates_in = signal("gates_in", 16 * 4)
        keys_in = signal("keys_in", 16)
        ss_ready = signal("ss_ready", len(NORMS))
        mid_ready = signal("mid_ready", len(NORMS))
        rstd_ready = signal("rstd_ready", len(NORMS))
        h_ready = signal("h_ready", 2 * NT)
        hT_ready = signal("hT_ready", 2 * NT)
        z0_ready = signal("z0_ready", NT)
        zq_ready = signal("zq_ready", NT)
        ckv_ready = signal("ckv_ready", NT)
        cq_ready = signal("cq_ready", NT)
        ckvT_ready = signal("ckvT_ready", NT)
        cqT_ready = signal("cqT_ready", NT)
        nope_in = signal("nope_in", NKT)
        ka_ready = signal("ka_ready", NKT)
        kaT_ready = signal("kaT_ready", NKT)
        u_in = signal("u_in", NT)
        qa_in = signal("qa_in", 2 * NT)
        qa_ready = signal("qa_ready", NT)
        v_in = signal("v_in", NT)
        v_ready = signal("v_ready", NT)
        ob_ready = signal("ob_ready", NT)
        qc_in = signal("qc_in", NT)
        qc_ready = signal("qc_ready", NT)
        kc_in = signal("kc_in", NT)
        kc_ready = signal("kc_ready", NT)
        kcT_ready = signal("kcT_ready", NT)
        latents_stored = signal("latents_stored", 32)
        kv_stored = signal("kv_stored", 32)
        qT_ready = signal("qT_ready", 2 * NT)
        max_ready = signal("max_ready", 2 * H * NT)
        exp_ready = signal("exp_ready", 2 * H * NT)
        pt_ready = signal("pt_ready", 2 * H * NT)
        o_done = signal("o_done", 2 * H * NT)
        o_moved = signal("o_moved", 2 * NT)
        oT_ready = signal("oT_ready", 2 * NT)
        sg_ready = signal("sg_ready", 6 * NT)
        merge_done = signal("merge_done", 6 * NT)
        mT_ready = signal("mT_ready", NT)
        pq_ready = signal("pq_ready", 16)
        scores_ready = signal("scores_ready", 16)
        cv_ready = signal("cv_ready", NT * TURNS + 1)
        ce_ready = signal("ce_ready", NT * TURNS + 1)
        half_ready = signal("half_ready", 2 * NT * TURNS + 1)
        g_land = [signal(f"g_land{r}", 16 * NT * SLOTS // RING) for r in range(RING)]
        dots_ready = signal("dots_ready", NT * SLOTS // GRP)
        gel_ready = signal("gel_ready", NT * SLOTS // GRP)
        wts_ready = signal("wts_ready", NT * SLOTS // GRP)
        diag_ready = signal("diag_ready", NT * SLOTS)
        slot_used = signal("slot_used", NT * SLOTS + RING)
        acc_full = signal("acc_full", NT)
        acc_used = signal("acc_used", NT)
        y_stored = signal("y_stored", 0)

        waits_passed = signal("waits_passed", 0)

        def alone(eng):
            eng.sem_inc(waits_passed.sem, 1)

        def unit_ap(l, n):
            _, at, size = UNO[n]
            row = ins["weights"][bass.ds(l, 1), at:at + P * size]
            return row.rearrange("a (p n) -> (a p) n", p=P)

        def unit_in(name, k, shape):
            i, _, size = UNO[name]
            return wring[i % NU][:, 0:size].rearrange("p (k n) -> p k n", k=shape)

        def one_of(step):
            return one[ONE_NO[step] % NB1]

        def pair_of(step):
            return pair[PAIR_NO[step] % NB2]

        block = ctx.enter_context(nc.Block())

        @block.sync
        def _(sp):
            with sp.Fori(0, L) as l:
                for n, (name, size) in enumerate(UNITS):
                    if n >= NU:
                        last = LAST_USE[UNITS[n - NU][0]]
                        if last in ONE_NO:
                            sp.wait_ge(one_full.sem, one_full.at(l, ONE_NO[last] + 1))
                            alone(sp)
                        else:
                            sp.wait_ge(pair_full.sem, pair_full.at(l, PAIR_NO[last] + 1))
                            alone(sp)
                    sp.dma_start(wring[n % NU][:, 0:size], unit_ap(l, name)).then_inc(w_land[n % NU].sem, 16)
                sp.drain().then_inc(layer_end.sem, 1)
                sp.wait_ge(layer_end.sem, layer_end.at(l, 5))
                alone(sp)
            for i in range(NT):
                dst = outs["y_prompt"][0] if i == 0 else outs["y_sample"][0, (i - 1) * P:i * P, :]
                sp.dma_start(dst, x[:, i, :]).then_inc(y_stored.sem, 16)
            sp.wait_ge(y_stored.sem, 16 * NT)

        @block.gpsimd
        def _(pool):
            nc.gpsimd.memset(zeros[:], 0.0)
            nc.gpsimd.memset(mhalf[:], -0.5)
            nc.gpsimd.memset(ones[:], 1.0)
            nc.gpsimd.memset(base[:], 0.0).then_inc(const_ready.sem, 1)
            pool.wait_ge(const_ready.sem, 1)
            alone(pool)
            for i in range(NT):
                pool.wait_ge(w_land[i].sem, 32)
                alone(pool)
                src = ins["x_prompt"][0] if i == 0 else ins["x_sample"][0, (i - 1) * P:i * P, :]
                pool.dma_start(x[:, i, :], src).then_inc(x_in.sem, 16)
            with pool.Fori(0, L) as l:
                for e, (key, cols, width) in enumerate(NORMS):
                    _, at, _, _ = NORM_AT[key]
                    pool.wait_ge(ss_ready.sem, ss_ready.at(l, e + 1))
                    alone(pool)
                    nc.gpsimd.tensor_scalar(ss[:, at:at + cols], ss[:, at:at + cols], 1.0 / width, EPS,
                                            ALU.mult, ALU.add).then_inc(mid_ready.sem, 1)
                    pool.wait_ge(mid_ready.sem, mid_ready.at(l, e + 1))
                    alone(pool)
                    nc.gpsimd.tensor_tensor(rstd[:, at:at + cols], ss[:, at:at + cols],
                                            mhalf[:].to_broadcast([P, cols]), ALU.pow).then_inc(rstd_ready.sem, 1)
                for i in range(NT):
                    with pool.Fori(0, TURNS) as t:
                        for s in range(BODY):
                            if s % HALF == 0:
                                pool.wait_ge(half_ready.sem, l * half_ready.layer + t * 2 + (2 * i * TURNS + s // HALF + 1))
                            pool.wait_ge(slot_used.sem, l * slot_used.layer + t * BODY + (i * SLOTS + s + 1))
                            alone(pool)
                            pool.indirect_dma_start(
                                out=ring[s % RING], out_offset=None, in_=ins["experts"],
                                in_offset=bass.IndirectOffsetOnAxis(ap=ihead[:, s:s + 1], axis=0)
                            ).then_inc(g_land[s % RING].sem, 16)
                pool.drain().then_inc(layer_end.sem, 1)
                pool.wait_ge(layer_end.sem, layer_end.at(l, 5))
                alone(pool)

        @block.tensor
        def _(pe):
            MM = nc.tensor.matmul
            TR = nc.tensor.transpose

            pe.wait_ge(cond_ready.sem, 2)
            pe.wait_ge(const_ready.sem, 1)
            with pe.Fori(0, L) as l:
                landed = set()

                def unit(name, k):
                    n = UNO[name][0]
                    if name not in landed:
                        landed.add(name)
                        pe.wait_ge(w_land[n % NU].sem, w_land[n % NU].at(l, 16 * (n // NU + 1)))
                    return unit_in(name, 0, k)

                def project(dst, i, name, cols):
                    for k in range(DK):
                        w = unit((name[0], name[1], k // 4), 4)
                        last = MM(dst[:, 0:cols], hT[:, k, i * P:(i + 1) * P], w[:, k % 4, :], start=k == 0, stop=k == DK - 1)
                    return last

                for step in STEPS:
                    kind, i = step[0], step[1]
                    if step in ONE_NO:
                        j = ONE_NO[step]
                        if j >= NB1:
                            pe.wait_ge(one_free[j % NB1].sem, one_free[j % NB1].at(l, j // NB1))
                        dst = one_of(step)
                    elif step in PAIR_NO:
                        j = PAIR_NO[step]
                        if j >= NB2:
                            pe.wait_ge(pair_free[j % NB2].sem, pair_free[j % NB2].at(l, j // NB2))
                        dst = pair_of(step)

                    if kind == "mod":
                        for k in range(DK):
                            w = unit(("mod", i, k // 4), 4)
                            last = MM(dst[0:2, :], cond[:, k, :], w[:, k % 4, :], start=k == 0, stop=k == DK - 1)
                        last.then_inc(one_full.sem, 1)
                    elif kind == "hT":
                        phase, i = step[1:]
                        if (phase, i) == (0, 0):
                            pe.wait_ge(const_in.sem, 16 * 3)
                        if (phase, i) == (1, NT - 1):
                            j = PAIR_NO[("pq", 0)]
                            pe.wait_ge(pair_free[j % NB2].sem, pair_free[j % NB2].at(l, j // NB2))
                            pe.wait_ge(hT_ready.sem, hT_ready.at(l, 2 * NT - 1))
                            w = unit(("pq", 0, 0), 16)
                            for k in range(DK):
                                MM(pair_of(("pq", 0))[:, 0:512], w[:, k, :], hT[:, k, 0:512], start=k == 0, stop=k == DK - 1)
                        pe.wait_ge(h_ready.sem, h_ready.at(l, phase * NT + i + 1))
                        src = h2[:, i, :] if phase else hbuf[i % 2]
                        for k in range(DK):
                            last = TR(dst[:, k * P:(k + 1) * P], src[:, k * P:(k + 1) * P], ident[:])
                        last.then_inc(pair_full.sem, 1)
                    elif kind in ("kv", "cq", "u", "v", "qc", "kc"):
                        if kind == "kv":
                            pe.wait_ge(hT_ready.sem, hT_ready.at(l, i + 1))
                        cols = {"kv": 288, "cq": QL, "kc": 256}.get(kind, 512)
                        project(dst, i, (kind, 0), cols).then_inc(one_full.sem, 1)
                    elif kind == "ckvT":
                        pe.wait_ge(ckv_ready.sem, ckv_ready.at(l, i + 1))
                        for k in range(2):
                            last = TR(dst[:, k * P:(k + 1) * P], z0[i][:, k * P:(k + 1) * P], ident[:])
                        last.then_inc(pair_full.sem, 1)
                    elif kind == "ukv":
                        half = step[2]
                        if i < NT:
                            pe.wait_ge(ckvT_ready.sem, ckvT_ready.at(l, i + 1))
                            src = latT[i % 2].rearrange("p (k t) -> p k t", k=3)
                        else:
                            pe.wait_ge(layer_in.sem, layer_in.at(l, layer_in.layer))
                            src = ckvT_ctx[:, :, (i - NT) * P:(i - NT + 1) * P]
                        w = unit(("ukv", 0, 0), 2)
                        for k in range(2):
                            last = MM(dst, src[:, k, :], w[:, k, half * 512:(half + 1) * 512], start=k == 0, stop=k == 1)
                        last.then_inc(one_full.sem, 1)
                    elif kind == "kaT":
                        pe.wait_ge(ka_ready.sem, ka_ready.at(l, i + 1))
                        for h in range(H):
                            last = TR(dst[0:AQK, h * P:(h + 1) * P], kbuf[i % 2][:, h * AQK:(h + 1) * AQK], ident[:])
                        last.then_inc(pair_full.sem, 1)
                    elif kind == "cqT":
                        pe.wait_ge(cq_ready.sem, cq_ready.at(l, i + 1))
                        for k in range(3):
                            last = TR(dst[:, k * P:(k + 1) * P], zq[i][:, k * P:(k + 1) * P], ident[:])
                        last.then_inc(pair_full.sem, 1)
                    elif kind == "uq":
                        pe.wait_ge(cqT_ready.sem, cqT_ready.at(l, i + 1))
                        w = unit(("uq", 0, step[2]), 3)
                        for k in range(3):
                            last = MM(dst[:, 0:384], latT[i % 2][:, k * P:(k + 1) * P], w[:, k, :], start=k == 0, stop=k == 2)
                        last.then_inc(one_full.sem, 1)
                    elif kind == "vm":
                        pe.wait_ge(v_ready.sem, v_ready.at(l, i + 1))
                        w = unit(("ws", 0, 0), H)
                        for g in range(H):
                            last = MM(dst[:, g * 64:(g + 1) * 64], w[:, g, :], vb[i][:, g * 64:(g + 1) * 64], start=True, stop=True)
                        last.then_inc(one_full.sem, 1)
                    elif kind == "kcT":
                        pe.wait_ge(kc_ready.sem, kc_ready.at(l, i + 1))
                        alone(pe)
                        for g in range(CKV):
                            last = TR(dst[0:CD, g * P:(g + 1) * P], kcb[i][:, g * CD:(g + 1) * CD], ident[:])
                        last.then_inc(pair_full.sem, 1)
                    elif kind == "qT":
                        t, m = divmod(i, 2)
                        if m == 0:
                            pe.wait_ge(qa_ready.sem, qa_ready.at(l, t + 1))
                            src, w = z[:, t, 1024:1792], AQK
                        else:
                            pe.wait_ge(qc_ready.sem, qc_ready.at(l, t + 1))
                            alone(pe)
                            src, w = z[:, t, 512:1024], CD
                        for h in range(H):
                            last = TR(dst[0:w, h * P:(h + 1) * P], src[:, h * w:(h + 1) * w], ident[:])
                        last.then_inc(pair_full.sem, 1)
                    elif kind == "s":
                        t, r = divmod(i, 2 * H)
                        m, h = divmod(r, H)
                        ks = unit_keys(i)
                        w, kT, g = (AQK, kaT, h) if m == 0 else (CD, kcT, h // (H // CKV))
                        if h == 0:
                            pe.wait_ge(qT_ready.sem, qT_ready.at(l, 2 * t + m + 1))
                        if i == 0:
                            pe.wait_ge(kaT_ready.sem, kaT_ready.at(l, NKT))
                        if i == H:
                            pe.wait_ge(kcT_ready.sem, kcT_ready.at(l, NT))
                            pe.wait_ge(layer_in.sem, layer_in.at(l, layer_in.layer))
                        q = qTb[m].rearrange("p (h t) -> p h t", h=H)[0:w, h, :]
                        c = 0
                        while c < len(ks):
                            n = 1
                            while c + n < len(ks) and ks[c + n] == ks[c] + n and (c + n) % 4:
                                n += 1
                            masks = [(c + d, int(ks[c + d] > t)) for d in range(n) if m and t and ks[c + d] < NT and ks[c + d] != t]
                            last = MM(dst[:, c * P:(c + n) * P], q, kT[:, g, ks[c] * P:(ks[c] + n) * P], start=True, stop=not masks)
                            for e, (pos, side) in enumerate(masks):
                                last = MM(dst[:, pos * P:(pos + 1) * P], ident[:], mask[:, side, :], start=False, stop=e == len(masks) - 1)
                            c += n
                        if m:
                            a = GAINS["sink"][0] + h
                            last = MM(dst[:, len(ks) * P:len(ks) * P + 1], ones[:], gains[0:1, a:a + 1], start=True, stop=True)
                        last.then_inc(pair_full.sem, 1)
                    elif kind == "PT":
                        pe.wait_ge(exp_ready.sem, exp_ready.at(l, i + 1))
                        for k in range(len(unit_keys(i))):
                            last = TR(dst[:, k * P:(k + 1) * P], pb[i % 2][:, k * P:(k + 1) * P], ident[:])
                        last.then_inc(pair_full.sem, 1)
                    elif kind == "O":
                        t, r = divmod(i, 2 * H)
                        m, h = divmod(r, H)
                        if i == 0:
                            for b in range(NB1):
                                n = sum(1 for s in ONES[:ONE_NO[("g", 0, 0)]] if ONE_NO[s] % NB1 == b)
                                pe.wait_ge(one_free[b].sem, one_free[b].at(l, n))
                        if h == 0 and t:
                            pe.wait_ge(o_moved.sem, o_moved.at(l, 2 * (t - 1) + m + 1))
                        pe.wait_ge(pt_ready.sem, pt_ready.at(l, i + 1))
                        ks = unit_keys(i)
                        for k, kt in enumerate(ks):
                            v = va[:, kt, h * 64:(h + 1) * 64] if m == 0 else vc[:, kt, h // (H // CKV) * CD:(h // (H // CKV) + 1) * CD]
                            last = MM(one[m][:, h * 64:(h + 1) * 64], ptb[i % 2][:, k * P:(k + 1) * P], v, start=k == 0, stop=k == len(ks) - 1)
                        last.then_inc(o_done.sem, 1)
                    elif kind == "oT":
                        pe.wait_ge(o_moved.sem, o_moved.at(l, 2 * i + 2))
                        if step[2] == 0:
                            pe.wait_ge(ob_ready.sem, ob_ready.at(l, i + 1))
                            blocks = [otok[:, k * P:(k + 1) * P] for k in range(4)] + [z[:, i, k * P:(k + 1) * P] for k in range(4)]
                        else:
                            blocks = [otok[:, 512 + k * P:512 + (k + 1) * P] for k in range(4)]
                        for k, src in enumerate(blocks):
                            last = TR(dst[:, k * P:(k + 1) * P], src, ident[:])
                        last.then_inc(pair_full.sem, 1)
                    elif kind == "g":
                        t = step[2]
                        if step == ("g", 0, 0):
                            pe.wait_ge(o_moved.sem, o_moved.at(l, 2 * NT))
                        project(dst, t, ("gate", i), 512).then_inc(one_full.sem, 1)
                    elif kind == "p":
                        t, b = step[2], i // 2
                        if i == 0:
                            pe.wait_ge(oT_ready.sem, oT_ready.at(l, 2 * t + 2))
                        w = unit(("proj", i, 0), 4)
                        for k in range(4):
                            last = MM(dst, oT[t][:, 4 * b + k, :], w[:, k, :], start=k == 0, stop=k == 3)
                        last.then_inc(one_full.sem, 1)
                    elif kind == "mT":
                        pe.wait_ge(merge_done.sem, merge_done.at(l, 5 * NT + i + 1))
                        for k in range(DK):
                            last = TR(dst[:, k * P:(k + 1) * P], merged[:, i, k * P:(k + 1) * P], ident[:])
                        last.then_inc(pair_full.sem, 1)
                    elif kind == "o":
                        pe.wait_ge(mT_ready.sem, mT_ready.at(l, i + 1))
                        for k in range(DK):
                            w = unit(("out", step[2], k // 4), 4)
                            last = MM(dst, mT[i % 2][:, k * P:(k + 1) * P], w[:, k % 4, :], start=k == 0, stop=k == DK - 1)
                        last.then_inc(one_full.sem, 1)
                    elif kind == "pq":
                        if i == 0:
                            pe.wait_ge(hT_ready.sem, hT_ready.at(l, 2 * NT))
                        w = unit(("pq", i // 2, 0), 16)
                        for a, b in ((0, 512), (512, NT * P))[i == 0:]:
                            for k in range(DK):
                                last = MM(dst[:, a:b], w[:, i % 2 * 8 + k, :], hT[:, k, a:b], start=k == 0, stop=k == DK - 1)
                        last.then_inc(pair_full.sem, 1)
                        if i % 2 and i // 2 >= 8 - NU:
                            r = i // 2 - (8 - NU)
                            pe.drain().then_inc(slot_used.sem, 1 if r < NU - 1 else RING - (NU - 1))
                    elif kind == "sc":
                        if i == 0:
                            pe.wait_ge(keys_in.sem, keys_in.at(l, 16))
                        pe.wait_ge(pq_ready.sem, pq_ready.at(l, i + 1))
                        for t in range(NT):
                            last = MM(dst[:, t * P:(t + 1) * P], pqT[:, t, i, :], keys[:, i, :], start=True, stop=True)
                        last.then_inc(pair_full.sem, 1)

                for i in range(NT):
                    a = acc[i % 2]
                    if i == 1:
                        for b in range(NB2):
                            pe.wait_ge(pair_free[b].sem, pair_free[b].at(l, pair_free[b].layer))
                    if i >= 2:
                        pe.wait_ge(acc_used.sem, acc_used.at(l, i - 1))
                    if i == 0:
                        for b in range(NB1):
                            pe.wait_ge(one_free[b].sem, one_free[b].at(l, one_free[b].layer))
                    for c in range(2):
                        MM(a[:, c * 512:(c + 1) * 512], zeros[:], h2[:, i, c * 512:(c + 1) * 512], start=True, stop=False)
                    with pe.Fori(0, TURNS) as t:
                        for s in range(BODY):
                            pe.wait_ge(diag_ready.sem, l * diag_ready.layer + t * BODY + (i * SLOTS + s + 1))
                            for c in range(2):
                                last = MM(a[:, c * 512:(c + 1) * 512], diag[s % RING], ring[s % RING][:, D + c * 512:D + (c + 1) * 512], start=False, stop=False)
                            last.then_inc(slot_used.sem, 1)
                    for c in range(2):
                        last = MM(a[:, c * 512:(c + 1) * 512], zeros[:], h2[:, i, c * 512:(c + 1) * 512], start=False, stop=True)
                    last.then_inc(acc_full.sem, 1)
                pe.drain().then_inc(layer_end.sem, 1)
                pe.wait_ge(layer_end.sem, layer_end.at(l, 5))

        @block.scalar
        def _(act):
            A = nc.scalar.activation

            act.dma_start(cond[:], ins["cond"]).then_inc(cond_in.sem, 16)
            act.dma_start(ident[:], ins["ident"]).then_inc(const_in.sem, 16)
            act.dma_start(mask[:], ins["mask"]).then_inc(const_in.sem, 16)
            act.dma_start(rope[:], ins["rope"]).then_inc(const_in.sem, 16)
            act.wait_ge(cond_in.sem, 16)
            A(sq[:, 0:2 * DK], cond[:].rearrange("p k s -> p (k s)"), ACT.Sigmoid).then_inc(cond_ready.sem, 1)
            with act.Fori(0, L) as l:
                row = lambda name: ins[name][bass.ds(l, 1)]
                act.dma_start(gains[:], row("gains").partition_broadcast(P).rearrange("p a n -> p (a n)")).then_inc(layer_in.sem, 16)
                act.dma_start(modrow, row("b_mod").partition_broadcast(2).rearrange("p a n -> p (a n)")).then_inc(layer_in.sem, 16)
                act.dma_start(bs[:], row("b_s").rearrange("a p n -> (a p) n")).then_inc(layer_in.sem, 16)
                act.dma_start(kcT[:, :, NT * P:], row("ctx_kT").rearrange("a p g t -> (a p) g t")).then_inc(layer_in.sem, 16)
                act.dma_start(vc[:, NT:, :], row("ctx_v").rearrange("a p t n -> (a p) t n")).then_inc(layer_in.sem, 16)
                act.dma_start(grow, row("g_norm")[:, 0:D].partition_broadcast(P).rearrange("p a n -> p (a n)")).then_inc(rows_in.sem, 16)
                act.wait_ge(mod_ready.sem, mod_ready.at(l, 1))
                act.dma_start(modd[:, 0:2 * D], modrow[:, 0:2 * D]).then_inc(mod_stored.sem, 16)
                act.wait_ge(mod_stored.sem, mod_stored.at(l, 16))
                for s in range(2):
                    for a, c in ((0, 1), (1, 0)):
                        act.dma_start(rows[:, s, a, :], modd[s:s + 1, c * D:(c + 1) * D].partition_broadcast(P).rearrange("p a n -> p (a n)")).then_inc(rows_in.sem, 16)

                for step in STEPS:
                    kind, i = step[0], step[1]
                    if step in ONE_NO:
                        full, j, src = one_full, ONE_NO[step], one_of(step)
                        freed = one_free[j % NB1]
                    elif step in PAIR_NO:
                        full, j, src = pair_full, PAIR_NO[step], pair_of(step)
                        freed = pair_free[j % NB2]

                    if kind == "hT":
                        phase, i = step[1:]
                        act.wait_ge(full.sem, full.at(l, j + 1))
                        A(hT[:, :, i * P:(i + 1) * P], src.rearrange("p (k t) -> p k t", k=DK), ACT.Copy).then_inc(freed.sem, 1)
                        act.drain().then_inc(hT_ready.sem, 1)
                        if step == ("hT", 0, NT - 1):
                            act.dma_start(ckvT_ctx, row("ctx_ckvT").rearrange("a p k t -> (a p) k t")).then_inc(layer_in.sem, 16)
                            act.dma_start(kr_ctx, row("ctx_kr").rearrange("a p n -> (a p) n")).then_inc(layer_in.sem, 16)
                    elif kind in ("kv", "cq", "qc"):
                        if step == ("kv", 0):
                            act.wait_ge(mod_ready.sem, mod_ready.at(l, 2))
                            act.dma_start(modd[:, 2 * D:], modrow[:, 2 * D:]).then_inc(mod_stored.sem, 16)
                        dst, ready = {"kv": (z0[i], z0_ready), "cq": (zq[i], zq_ready), "qc": (z[:, i, 512:1024], qc_in)}[kind]
                        act.wait_ge(full.sem, full.at(l, j + 1))
                        A(dst, src[:, 0:dst.shape[1]], ACT.Copy).then_inc(freed.sem, 1)
                        act.drain().then_inc(ready.sem, 1)
                        if step == ("cq", NT - 1):
                            act.wait_ge(ckv_ready.sem, ckv_ready.at(l, 1))
                            act.dma_start(outs["new_mla_ckv"][0, bass.ds(l, 1)].rearrange("a p n -> (a p) n"), z0[0][:, 0:KVL]).then_inc(latents_stored.sem, 16)
                            act.dma_start(outs["new_mla_krope"][0, bass.ds(l, 1)].rearrange("a p n -> (a p) n"), z0[0][:, KVL:288]).then_inc(latents_stored.sem, 16)
                            act.wait_ge(mod_stored.sem, mod_stored.at(l, 32))
                    elif kind == "ckvT":
                        act.wait_ge(full.sem, full.at(l, j + 1))
                        A(latT[i % 2][:, 0:256], src[:, 0:256], ACT.Copy).then_inc(freed.sem, 1)
                        act.drain().then_inc(ckvT_ready.sem, 1)
                    elif kind == "ukv":
                        act.wait_ge(full.sem, full.at(l, j + 1))
                        if step[2] == 0:
                            if i >= 2:
                                act.wait_ge(pair_full.sem, pair_full.at(l, PAIR_NO[("kaT", i - 2)] + 1))
                            A(kbuf[i % 2].rearrange("p (h n) -> p h n", h=H)[:, :, 0:NOPE], src.rearrange("p (h n) -> p h n", h=H), ACT.Copy).then_inc(freed.sem, 1)
                            act.drain().then_inc(nope_in.sem, 1)
                        else:
                            A(va[:, i, :], src, ACT.Copy).then_inc(freed.sem, 1)
                    elif kind == "kaT":
                        act.wait_ge(full.sem, full.at(l, j + 1))
                        A(kaT[:, :, i * P:(i + 1) * P], src[0:AQK, :].rearrange("p (h t) -> p h t", h=H), ACT.Copy).then_inc(freed.sem, 1)
                        act.drain().then_inc(kaT_ready.sem, 1)
                    elif kind == "u":
                        act.wait_ge(full.sem, full.at(l, j + 1))
                        A(z[:, i, 0:512], src, ACT.Gelu_apprx_tanh).then_inc(freed.sem, 1)
                        act.drain().then_inc(u_in.sem, 1)
                    elif kind == "cqT":
                        act.wait_ge(full.sem, full.at(l, j + 1))
                        A(latT[i % 2], src[:, 0:QL], ACT.Copy).then_inc(freed.sem, 1)
                        act.drain().then_inc(cqT_ready.sem, 1)
                    elif kind == "uq":
                        act.wait_ge(full.sem, full.at(l, j + 1))
                        A(z[:, i, 1024 + 384 * step[2]:1024 + 384 * (step[2] + 1)], src[:, 0:384], ACT.Copy).then_inc(freed.sem, 1)
                        act.drain().then_inc(qa_in.sem, 1)
                    elif kind == "v":
                        if i == 0:
                            act.wait_ge(ka_ready.sem, ka_ready.at(l, NKT))
                            act.wait_ge(latents_stored.sem, latents_stored.at(l, 32))
                        act.wait_ge(full.sem, full.at(l, j + 1))
                        A(vb[i], src, ACT.Gelu_apprx_tanh).then_inc(freed.sem, 1)
                        act.drain().then_inc(v_in.sem, 1)
                    elif kind == "kc":
                        act.wait_ge(full.sem, full.at(l, j + 1))
                        A(kcb[i], src[:, 0:128], ACT.Copy)
                        A(vc[:, i, :], src[:, 128:256], ACT.Copy).then_inc(freed.sem, 1)
                        act.drain().then_inc(kc_in.sem, 1)
                    elif kind == "kcT":
                        act.wait_ge(full.sem, full.at(l, j + 1))
                        A(kcT[:, :, i * P:(i + 1) * P], src[0:CD, 0:256].rearrange("p (g t) -> p g t", g=CKV), ACT.Copy).then_inc(freed.sem, 1)
                        act.drain().then_inc(kcT_ready.sem, 1)
                        if i == 0:
                            act.dma_start(outs["new_swa_k"][0, bass.ds(l, 1)].rearrange("a p g n -> (a p) (g n)"), kcb[0]).then_inc(kv_stored.sem, 16)
                            act.dma_start(outs["new_swa_v"][0, bass.ds(l, 1)].rearrange("a p g n -> (a p) (g n)"), vc[:, 0, :]).then_inc(kv_stored.sem, 16)
                    elif kind == "qT":
                        w = AQK if i % 2 == 0 else CD
                        act.wait_ge(full.sem, full.at(l, j + 1))
                        A(qTb[i % 2][0:w, :], src[0:w, :], ACT.Copy).then_inc(freed.sem, 1)
                        act.drain().then_inc(qT_ready.sem, 1)
                    elif kind == "s":
                        n = len(unit_keys(i)) * P + i % (2 * H) // H
                        if i == 0:
                            act.wait_ge(kv_stored.sem, kv_stored.at(l, 32))
                        act.wait_ge(max_ready.sem, max_ready.at(l, i + 1))
                        if i >= 2:
                            act.wait_ge(pair_full.sem, pair_full.at(l, PAIR_NO[("PT", i - 2)] + 1))
                        A(pb[i % 2][:, 0:n], src[:, 0:n], ACT.Exp, bias=negm[:, i:i + 1], accum_out=rsum[:, i:i + 1]).then_inc(freed.sem, 1)
                        act.drain().then_inc(exp_ready.sem, 1)
                    elif kind == "oT":
                        n = 8 if step[2] == 0 else 4
                        act.wait_ge(full.sem, full.at(l, j + 1))
                        A(oT[i][:, 8 * step[2]:8 * step[2] + n, :], src[:, 0:n * P].rearrange("p (k t) -> p k t", k=n), ACT.Copy).then_inc(freed.sem, 1)
                        act.drain().then_inc(oT_ready.sem, 1)
                        if step == ("oT", NT - 1, 1):
                            act.dma_start(grow2, row("g_norm")[:, D:2 * D].partition_broadcast(P).rearrange("p a n -> p (a n)")).then_inc(rows_in.sem, 16)
                            for s in range(2):
                                for dst, c in ((scale2, 4), (shift2, 3)):
                                    act.dma_start(dst[:, s, :], modd[s:s + 1, c * D:(c + 1) * D].partition_broadcast(P).rearrange("p a n -> p (a n)")).then_inc(rows_in.sem, 16)
                            for s in range(2):
                                for dst, c in ((g1, 2), (g2, 5)):
                                    act.dma_start(dst[:, s, :], modd[s:s + 1, c * D:(c + 1) * D].partition_broadcast(P).rearrange("p a n -> p (a n)")).then_inc(gates_in.sem, 16)
                    elif kind == "g":
                        n = i * NT + step[2]
                        act.wait_ge(full.sem, full.at(l, j + 1))
                        if n >= 2:
                            act.wait_ge(merge_done.sem, merge_done.at(l, n - 1))
                        A(sg[n % 2], src, ACT.Sigmoid).then_inc(freed.sem, 1)
                        act.drain().then_inc(sg_ready.sem, 1)
                    elif kind == "mT":
                        act.wait_ge(full.sem, full.at(l, j + 1))
                        if i >= 2:
                            act.wait_ge(one_full.sem, one_full.at(l, ONE_NO[("o", i - 2, 1)] + 1))
                        A(mT[i % 2], src, ACT.Copy).then_inc(freed.sem, 1)
                        act.drain().then_inc(mT_ready.sem, 1)
                        if i == 0:
                            act.dma_start(keys, row("keysT").rearrange("a p q n -> (a p) q n")).then_inc(keys_in.sem, 16)
                    elif kind == "pq":
                        act.wait_ge(full.sem, full.at(l, j + 1))
                        A(pqT[:, :, i, :], src[:, 0:NT * P].rearrange("p (t n) -> p t n", t=NT), ACT.Copy).then_inc(freed.sem, 1)
                        act.drain().then_inc(pq_ready.sem, 1)
                        if i == 8:
                            act.wait_ge(cv_ready.sem, cv_ready.at(l, 1))
                            A(gnext, gnext, ACT.Exp).then_inc(ce_ready.sem, 1)
                    elif kind == "sc":
                        act.wait_ge(full.sem, full.at(l, j + 1))
                        A(pqT[:, :, i, :], src[:, 0:NT * P].rearrange("p (t n) -> p t n", t=NT), ACT.Copy).then_inc(freed.sem, 1)
                        act.drain().then_inc(scores_ready.sem, 1)

                for i in range(NT):
                    with act.Fori(0, TURNS) as t:
                        for g in range(NGRP + 1):
                            n = i * SLOTS // GRP + g
                            if g < NGRP:
                                act.wait_ge(dots_ready.sem, l * dots_ready.layer + t * NGRP + (n + 1))
                                A(gel[:, g * GRP:(g + 1) * GRP], dots[:, g * GRP:(g + 1) * GRP], ACT.Gelu_apprx_tanh).then_inc(gel_ready.sem, 1)
                            if g:
                                act.wait_ge(wts_ready.sem, l * wts_ready.layer + t * NGRP + n)
                                for s in range((g - 1) * GRP, g * GRP):
                                    act.wait_ge(slot_used.sem, l * slot_used.layer + t * BODY + (i * SLOTS + s + 1))
                                    A(diag[s % RING], ident[:], ACT.Copy, scale=wts[:, s:s + 1]).then_inc(diag_ready.sem, 1)
                            if g == 5:
                                act.wait_ge(cv_ready.sem, l * cv_ready.layer + t + (i * TURNS + 2))
                                A(gnext, gnext, ACT.Exp).then_inc(ce_ready.sem, 1)
                act.drain().then_inc(layer_end.sem, 1)
                act.wait_ge(layer_end.sem, layer_end.at(l, 5))

        @block.vector
        def _(dve):
            V = nc.vector
            TT, TS, STT = V.tensor_tensor, V.tensor_scalar, V.scalar_tensor_tensor
            dve.wait_ge(cond_ready.sem, 1)
            cflat = cond[:].rearrange("p k s -> p (k s)")
            TT(cflat, cflat, sq[:, 0:2 * DK], ALU.mult).then_inc(cond_ready.sem, 1)
            dve.wait_ge(const_in.sem, 16 * 3)
            dve.wait_ge(const_ready.sem, 1)

            with dve.Fori(0, L) as l:

                def gain(name, heads):
                    a, n = GAINS[name]
                    return gains[:, a:a + n].unsqueeze(1).to_broadcast([P, heads, n])

                def stat(key):
                    e, at, cols, _ = NORM_AT[key]
                    return e, ss[:, at:at + cols], rstd[:, at:at + cols]

                def squares(key, src, width):
                    e, s, _ = stat(key)
                    V.tensor_tensor_reduce(out=sq[:, 0:width], in0=src, in1=src, scale=1.0, scalar=0.0,
                                           op0=ALU.mult, op1=ALU.add, accum_out=s).then_inc(ss_ready.sem, 1)

                def head_squares(key, src3, heads, n):
                    e, s, _ = stat(key)
                    t = sq[:, 0:heads * n].rearrange("p (h n) -> p h n", h=heads)
                    TT(t, src3, src3, ALU.mult)
                    dve.drain()
                    V.tensor_reduce(s, t, AX.X, ALU.add).then_inc(ss_ready.sem, 1)

                def wait_rstd(key):
                    e, _, r = stat(key)
                    dve.wait_ge(rstd_ready.sem, rstd_ready.at(l, e + 1))
                    return r

                def head_norm(key, src3, heads, n, gname):
                    r = wait_rstd(key)
                    TT(src3, src3, r.unsqueeze(2).to_broadcast([P, heads, n]), ALU.mult)
                    dve.drain()
                    TT(src3, src3, gain(gname, heads), ALU.mult)
                    dve.drain()

                def rotate(src3, heads, half, tile, at):
                    c = rope[:, tile - 1, at:at + half].unsqueeze(1).to_broadcast([P, heads, half])
                    s = rope[:, tile - 1, at + half:at + 2 * half].unsqueeze(1).to_broadcast([P, heads, half])
                    a, b = src3[:, :, 0:half], src3[:, :, half:2 * half]
                    t = sq[:, 0:2 * heads * half].rearrange("p (e h n) -> p e h n", e=2, h=heads)
                    TT(t[:, 0], a, s, ALU.mult)
                    TT(t[:, 1], b, s, ALU.mult)
                    dve.drain()
                    TT(a, a, c, ALU.mult)
                    TT(b, b, c, ALU.mult)
                    dve.drain()
                    TT(a, a, t[:, 1], ALU.subtract)
                    TT(b, b, t[:, 0], ALU.add)
                    dve.drain()

                def row_squares(i, dst):
                    return V.tensor_tensor_reduce(out=sq[:], in0=x[:, i, :], in1=x[:, i, :], scale=1.0, scalar=0.0,
                                                  op0=ALU.mult, op1=ALU.add, accum_out=dst)

                def modulate(dst, i, r, scale, shift):
                    st = min(i, 1)
                    STT(dst, x[:, i, :], r, scale[:, st, :], ALU.mult, ALU.mult)
                    dve.drain()
                    TT(dst, dst, shift[:, st, :], ALU.add).then_inc(h_ready.sem, 1)

                dve.wait_ge(layer_in.sem, layer_in.at(l, 80))
                for name, d in (("qa", AQK), ("qc", CD)):
                    a, n = GAINS[name]
                    TS(gains[:, a:a + n], gains[:, a:a + n], float(d) ** -0.5, None, ALU.mult)
                for b in range(12):
                    j = ONE_NO[("mod", b)]
                    dve.wait_ge(one_full.sem, one_full.at(l, j + 1))
                    last = TT(modrow[:, b * 512:(b + 1) * 512], one_of(("mod", b))[0:2, :], modrow[:, b * 512:(b + 1) * 512], ALU.add)
                    last.then_inc(one_free[j % NB1].sem, 1)
                    if b == 3:
                        dve.drain().then_inc(mod_ready.sem, 1)
                    if b in (3, 4):
                        if b == 3:
                            dve.wait_ge(x_in.sem, 16 * NT)
                        _, s, _ = stat(("n", 0))
                        for i in ((0, 1), (2, 3, 4))[b - 3]:
                            last = row_squares(i, s[:, i:i + 1])
                            if i < NT - 1:
                                dve.drain()
                        if b == 4:
                            last.then_inc(ss_ready.sem, 1)
                    elif b == HEAD - 2:
                        dve.wait_ge(rows_in.sem, rows_in.at(l, 80))
                        for st in range(2):
                            STT(rows[:, st, 0, :], rows[:, st, 0, :], 1.0, grow, ALU.add, ALU.mult)
                        dve.drain()
                    elif HEAD - 1 <= b < HEAD - 1 + NT:
                        i = b - (HEAD - 1)
                        r = wait_rstd(("n", 0))
                        if i >= 2:
                            dve.wait_ge(pair_full.sem, pair_full.at(l, PAIR_NO[("hT", 0, i - 2)] + 1))
                        modulate(hbuf[i % 2], i, r[:, i:i + 1], rows[:, :, 0, :], rows[:, :, 1, :])
                dve.drain().then_inc(mod_ready.sem, 1)

                for i in range(NT):
                    dve.wait_ge(z0_ready.sem, z0_ready.at(l, i + 1))
                    squares(("ckv", i), z0[i][:, 0:KVL], KVL)
                    dve.drain()
                a, n = GAINS["kv"]
                for i in range(NT):
                    r = wait_rstd(("ckv", i))
                    STT(z0[i][:, 0:KVL], z0[i][:, 0:KVL], r, gains[:, a:a + n], ALU.mult, ALU.mult).then_inc(ckv_ready.sem, 1)
                for i in range(NT):
                    dve.wait_ge(zq_ready.sem, zq_ready.at(l, i + 1))
                    squares(("cq", i), zq[i], QL)
                    dve.drain()
                a, n = GAINS["q"]
                for i in range(NT):
                    r = wait_rstd(("cq", i))
                    STT(zq[i], zq[i], r, gains[:, a:a + n], ALU.mult, ALU.mult).then_inc(cq_ready.sem, 1)

                for i in range(NKT):
                    k3 = kbuf[i % 2].rearrange("p (h n) -> p h n", h=H)
                    if i < NT:
                        kr = z0[i][:, KVL:288]
                    else:
                        if i == NT:
                            dve.wait_ge(layer_in.sem, layer_in.at(l, layer_in.layer))
                        kr = kr_ctx[:, (i - NT) * ROPE:(i - NT + 1) * ROPE]
                    dve.wait_ge(nope_in.sem, nope_in.at(l, i + 1))
                    V.tensor_copy(k3[:, :, NOPE:], kr.unsqueeze(1).to_broadcast([P, H, ROPE]))
                    dve.drain()
                    head_squares(("ka", i), k3, H, AQK)
                    head_norm(("ka", i), k3, H, AQK, "ka")
                    if 1 <= i < NT:
                        rotate(k3[:, :, NOPE:], H, ROPE // 2, i, 0)
                    dve.drain().then_inc(ka_ready.sem, 1)

                for i in range(NT + 1):
                    if i < NT:
                        dve.wait_ge(qa_in.sem, qa_in.at(l, 2 * i + 2))
                        head_squares(("qa", i), z[:, i, 1024:1792].rearrange("p (h n) -> p h n", h=H), H, AQK)
                        dve.drain()
                    if i:
                        q3 = z[:, i - 1, 1024:1792].rearrange("p (h n) -> p h n", h=H)
                        head_norm(("qa", i - 1), q3, H, AQK, "qa")
                        if i > 1:
                            rotate(q3[:, :, NOPE:], H, ROPE // 2, i - 1, 0)
                        dve.drain().then_inc(qa_ready.sem, 1)

                a, n = GAINS["v"]
                for i in range(NT + 1):
                    if i < NT:
                        dve.wait_ge(v_in.sem, v_in.at(l, i + 1))
                        squares(("v", i), vb[i], 512)
                        dve.drain()
                    if i:
                        r = wait_rstd(("v", i - 1))
                        STT(vb[i - 1], vb[i - 1], r, gains[:, a:a + n], ALU.mult, ALU.mult).then_inc(v_ready.sem, 1)
                for i in range(NT):
                    k3 = kcb[i].rearrange("p (h n) -> p h n", h=CKV)
                    dve.wait_ge(kc_in.sem, kc_in.at(l, i + 1))
                    head_squares(("kc", i), k3, CKV, CD)
                    dve.drain()
                for i in range(NT):
                    j = ONE_NO[("vm", i)]
                    dve.wait_ge(u_in.sem, u_in.at(l, i + 1))
                    dve.wait_ge(one_full.sem, one_full.at(l, j + 1))
                    t = sq[:, 0:512].rearrange("p (g n) -> p g n", g=H)
                    TT(t, one_of(("vm", i)).rearrange("p (g n) -> p g n", g=H), bs[:].unsqueeze(2).to_broadcast([P, H, 64]), ALU.add).then_inc(one_free[j % NB1].sem, 1)
                    dve.drain()
                    TT(z[:, i, 0:512], z[:, i, 0:512], sq[:, 0:512], ALU.mult).then_inc(ob_ready.sem, 1)
                    dve.drain()

                for i in range(NT):
                    k3 = kcb[i].rearrange("p (h n) -> p h n", h=CKV)
                    head_norm(("kc", i), k3, CKV, CD, "kc")
                    if i:
                        rotate(k3, CKV, CD // 2, i, 32)
                    dve.drain().then_inc(kc_ready.sem, 1)

                def query_squares(i):
                    dve.wait_ge(qc_in.sem, qc_in.at(l, i + 1))
                    head_squares(("qc", i), z[:, i, 512:1024].rearrange("p (h n) -> p h n", h=H), H, CD)
                    dve.drain()

                def query_norm(i):
                    head_norm(("qc", i), z[:, i, 512:1024].rearrange("p (h n) -> p h n", h=H), H, CD, "qc")

                def query_turn(i):
                    if i:
                        rotate(z[:, i, 512:1024].rearrange("p (h n) -> p h n", h=H), H, CD // 2, i, 32)
                    dve.drain().then_inc(qc_ready.sem, 1)

                for i in range(NT - 1):
                    query_squares(i)
                    if i:
                        query_norm(i - 1)
                        query_turn(i - 1)
                query_norm(NT - 2)
                query_turn(NT - 2)

                for step in STEPS:
                    kind, i = step[0], step[1]
                    if kind == "s":
                        n = len(unit_keys(i)) * P + i % (2 * H) // H
                        dve.wait_ge(pair_full.sem, pair_full.at(l, PAIR_NO[step] + 1))
                        V.tensor_reduce(negm[:, i:i + 1], pair_of(step)[:, 0:n], AX.X, ALU.max, negate=True).then_inc(max_ready.sem, 1)
                        if i == 2 * H + 2:
                            query_squares(NT - 1)
                        elif i == 2 * H + 3:
                            query_norm(NT - 1)
                        elif i == 2 * H + 4:
                            query_turn(NT - 1)
                    elif kind == "PT":
                        n = len(unit_keys(i)) * P
                        j = PAIR_NO[step]
                        dve.wait_ge(pair_full.sem, pair_full.at(l, j + 1))
                        if i >= 2:
                            dve.wait_ge(o_done.sem, o_done.at(l, i - 1))
                        V.tensor_copy(ptb[i % 2][:, 0:n], pair_of(step)[:, 0:n]).then_inc(pair_free[j % NB2].sem, 1)
                        dve.drain().then_inc(pt_ready.sem, 1)
                    elif kind == "O" and i % H == H - 1:
                        t, m = divmod(i // H, 2)
                        r = rsum[:, i - H + 1:i + 1]
                        dve.wait_ge(o_done.sem, o_done.at(l, i + 1))
                        V.reciprocal(r, r)
                        dve.drain()
                        if m == 0 and t:
                            dve.wait_ge(pair_full.sem, pair_full.at(l, PAIR_NO[("oT", t - 1, 1)] + 1))
                        TT(otok[:, 512 * m:512 * (m + 1)].rearrange("p (h n) -> p h n", h=H),
                           one[m].rearrange("p (h n) -> p h n", h=H), r.unsqueeze(2).to_broadcast([P, H, 64]), ALU.mult).then_inc(o_moved.sem, 1)
                    elif kind == "p":
                        bc, t = step[1:]
                        b, c = divmod(bc, 2)
                        n = bc * NT + t
                        j = ONE_NO[step]
                        dve.wait_ge(sg_ready.sem, sg_ready.at(l, n + 1))
                        dve.wait_ge(one_full.sem, one_full.at(l, j + 1))
                        m = merged[:, t, c * 512:(c + 1) * 512]
                        if b == 0:
                            TT(m, one_of(step), sg[n % 2], ALU.mult).then_inc(one_free[j % NB1].sem, 1)
                            dve.drain().then_inc(merge_done.sem, 1)
                        else:
                            TT(sq[:, 0:512], one_of(step), sg[n % 2], ALU.mult).then_inc(one_free[j % NB1].sem, 1)
                            dve.drain()
                            TT(m, m, sq[:, 0:512], ALU.add).then_inc(merge_done.sem, 1)
                            dve.drain()
                    elif kind == "o":
                        c = step[2]
                        j = ONE_NO[step]
                        if i == 0 and c == 0:
                            dve.wait_ge(gates_in.sem, gates_in.at(l, 64))
                            dve.wait_ge(rows_in.sem, rows_in.at(l, 160))
                            for st in range(2):
                                STT(scale2[:, st, :], scale2[:, st, :], 1.0, grow2, ALU.add, ALU.mult)
                            dve.drain()
                        dve.wait_ge(one_full.sem, one_full.at(l, j + 1))
                        TT(sq[:, 0:512], one_of(step), g1[:, min(i, 1), c * 512:(c + 1) * 512], ALU.mult).then_inc(one_free[j % NB1].sem, 1)
                        dve.drain()
                        xs = x[:, i, c * 512:(c + 1) * 512]
                        TT(xs, xs, sq[:, 0:512], ALU.add)
                        dve.drain()
                        if c == 1:
                            row_squares(i, stat(("n", 1, i))[1]).then_inc(ss_ready.sem, 1)
                            dve.drain()
                        if c == 0 and i:
                            modulate(h2[:, i - 1, :], i - 1, wait_rstd(("n", 1, i - 1)), scale2, shift2)
                            dve.drain()
                        if step == ("o", NT - 1, 1):
                            modulate(h2[:, i, :], i, wait_rstd(("n", 1, i)), scale2, shift2)
                            dve.drain()

                V.memset(iota, 0.0)
                dve.drain()
                for w in (1, 2, 4, 8):
                    TS(iota[:, w:2 * w], iota[:, 0:w], float(w), None, ALU.add)
                    dve.drain()

                def top16(vals, inds, src, tmp):
                    V.max(vals[:, 0:8], src)
                    dve.drain()
                    V.max_index(inds[:, 0:8], vals[:, 0:8], src)
                    V.match_replace(tmp, vals[:, 0:8], src, LOW)
                    dve.drain()
                    V.max(vals[:, 8:16], tmp)
                    dve.drain()
                    V.max_index(inds[:, 8:16], vals[:, 8:16], tmp)

                def choose_keys(turn, part):
                    if part == 0:
                        V.tensor_copy(sc4, big[:, bass.ds(turn * 512, 512)])
                        dve.drain()
                    for q in range(2 * part, 2 * part + 2):
                        top16(v16[:, q * 16:(q + 1) * 16], i16[:, q * 16:(q + 1) * 16], sc4[:, q * P:(q + 1) * P], tmpk[q % 2][:, 0:P])
                    dve.drain()

                v4 = v16.rearrange("p (h e k) -> p h e k", h=2, e=2)
                c4 = cand.rearrange("p (h a b) -> p h a b", h=2, a=16)
                g3 = gnext.rearrange("p (h k) -> p h k", h=2)
                cv3 = cv.rearrange("p (h k) -> p h k", h=2)
                wide = [P, 2, 16, 16]

                def choose_pairs(h):
                    if h == 0:
                        TT(c4, v4[:, :, 0, :].unsqueeze(3).to_broadcast(wide), v4[:, :, 1, :].unsqueeze(2).to_broadcast(wide), ALU.add)
                        V.tensor_copy(i16f, i16)
                        dve.drain()
                    top16(cv[:, h * 16:(h + 1) * 16], ci[:, h * 16:(h + 1) * 16], cand[:, h * 256:(h + 1) * 256], tmpk[h])
                    dve.drain()
                    if h == 0:
                        return
                    TT(g3, cv3, cv3[:, :, 0:1].to_broadcast([P, 2, 16]), ALU.subtract)
                    TS(cab[:, 0:BODY], ci, 4, None, ALU.logical_shift_right)
                    TS(cab[:, BODY:2 * BODY], ci, 15, None, ALU.bitwise_and)
                    dve.drain().then_inc(cv_ready.sem, 1)
                    V.tensor_copy(cabf, cab)
                    dve.drain()

                def choose_rows(e):
                    pos = cabf[:, e * BODY:(e + 1) * BODY].rearrange("p (h k) -> p h k", h=2)
                    fi = i16f.rearrange("p (h e k) -> p h e k", h=2, e=2)
                    TT(c4, pos.unsqueeze(3).to_broadcast(wide), iota.unsqueeze(1).unsqueeze(1).to_broadcast(wide), ALU.is_equal)
                    dve.drain()
                    TT(c4, c4, fi[:, :, e, :].unsqueeze(2).to_broadcast(wide), ALU.mult)
                    dve.drain()
                    V.tensor_reduce(sel[:, e * BODY:(e + 1) * BODY], cand.rearrange("p (n a) -> p n a", a=16), AX.X, ALU.add)
                    dve.drain()

                def choose_gates(count):
                    STT(sel[:, 0:BODY], sel[:, 0:BODY], 128.0, sel[:, BODY:2 * BODY], ALU.mult, ALU.add)
                    dve.wait_ge(ce_ready.sem, count)
                    V.tensor_reduce(esum, g3, AX.X, ALU.add)
                    dve.drain()
                    TS(inext, sel[:, 0:BODY], base[:], None, ALU.add)
                    V.reciprocal(esum, esum)
                    dve.drain()
                    TT(g3, g3, esum.unsqueeze(2).to_broadcast([P, 2, 16]), ALU.mult)
                    dve.drain()

                def refill(half):
                    a, b = half * HALF, (half + 1) * HALF
                    V.tensor_copy(ihead[:, a:b], inext[:, a:b])
                    V.tensor_copy(ghead[:, a:b], gnext[:, a:b])
                    dve.drain().then_inc(half_ready.sem, 1)

                def add_experts(i):
                    dve.wait_ge(acc_full.sem, acc_full.at(l, i + 1))
                    TT(sq[:], acc[i % 2], g2[:, min(i, 1), :], ALU.mult).then_inc(acc_used.sem, 1)
                    dve.drain()
                    TT(x[:, i, :], x[:, i, :], sq[:], ALU.add)
                    dve.drain()

                dve.wait_ge(scores_ready.sem, scores_ready.at(l, 4))
                choose_keys(0, 0)
                choose_keys(0, 1)
                choose_pairs(0)
                choose_pairs(1)
                choose_rows(0)
                choose_rows(1)
                choose_gates(ce_ready.at(l, 1))
                refill(0)
                for i in range(NT):
                    with dve.Fori(0, TURNS) as t:
                        dve.drain()
                        refill(1)
                        for g in range(NGRP + 1):
                            n = i * SLOTS // GRP + g
                            if g < NGRP:
                                for s in range(g * GRP, (g + 1) * GRP):
                                    r = s % RING
                                    dve.wait_ge(g_land[r].sem, l * g_land[r].layer + t * (16 * BODY // RING) + 16 * (i * SLOTS // RING + s // RING + 1))
                                    last = V.tensor_tensor_reduce(out=sq[:], in0=ring[r][:, 0:D], in1=h2[:, i, :], scale=1.0, scalar=0.0,
                                                                  op0=ALU.mult, op1=ALU.add, accum_out=dots[:, s:s + 1])
                                    if s % GRP < GRP - 1:
                                        dve.drain()
                                last.then_inc(dots_ready.sem, 1)
                                dve.drain()
                            if g:
                                dve.wait_ge(gel_ready.sem, l * gel_ready.layer + t * NGRP + n)
                                a, b = (g - 1) * GRP, g * GRP
                                TT(wts[:, a:b], gel[:, a:b], ghead[:, a:b], ALU.mult).then_inc(wts_ready.sem, 1)
                            if g in (1, 2):
                                if g == 1:
                                    dve.wait_ge(scores_ready.sem, scores_ready.at(l, 16))
                                choose_keys(t + (i * TURNS + 1), g - 1)
                            elif g in (3, 4):
                                choose_pairs(g - 3)
                            elif g in (5, 6):
                                choose_rows(g - 5)
                            elif g == 8:
                                choose_gates(l * ce_ready.layer + t + (i * TURNS + 2))
                            elif g == REFILL:
                                dve.drain()
                                refill(0)
                    if i:
                        add_experts(i - 1)
                add_experts(NT - 1)
                TS(base[:], base[:], float(NEXP), None, ALU.add)
                dve.drain().then_inc(layer_end.sem, 1)
                dve.wait_ge(layer_end.sem, layer_end.at(l, 5))


def lay_out(inputs):
    import numpy as np

    a = {k: np.ascontiguousarray(v) for k, v in inputs.items()}

    def unit(l, name):
        kind, b, k = name
        blocks = lambda w: w.reshape(-1, P, w.shape[1]).transpose(1, 0, 2)
        w_in = a["w_in"][l]
        first = {"cq": (0, 384), "kv": (384, 672), "u": (672, 1184), "v": (1184, 1696), "qc": (1696, 2208), "kc": (2208, 2464)}
        if kind in first:
            lo, hi = first[kind]
            return blocks(w_in[512 * k:512 * (k + 1), lo:hi])
        if kind == "mod":
            return blocks(a["w_mod"][l][512 * k:512 * (k + 1), 512 * b:512 * (b + 1)])
        if kind == "gate":
            return blocks(w_in[512 * k:512 * (k + 1), 2464 + 512 * b:2464 + 512 * (b + 1)])
        if kind == "proj":
            w = a[("w_o_a", "w_o_b", "w_o_c")[b // 2]][l]
            return blocks(w[:, 512 * (b % 2):512 * (b % 2 + 1)])
        if kind == "out":
            return blocks(a["w_out"][l][512 * k:512 * (k + 1), 512 * b:512 * (b + 1)])
        if kind == "ukv":
            w = a["w_ukv"][l].reshape(KVL, H, 2, 64).transpose(0, 2, 1, 3).reshape(KVL, D)
            return blocks(w)
        if kind == "uq":
            return blocks(a["w_uq"][l][:, 384 * k:384 * (k + 1)])
        if kind == "ws":
            return a["w_s_b"][l].transpose(2, 0, 1)
        if kind == "pq":
            w = a["w_pq"][l][:, 256 * b:256 * (b + 1)].reshape(DK, P, 2, P)
            return w.transpose(1, 2, 0, 3)

    r = {"x_prompt": a["x_prompt"], "x_sample": a["x_sample"]}
    weights = np.empty((L, WTOTAL), np.float32)
    for l in range(L):
        for name, (_, at, size) in UNO.items():
            weights[l, at:at + P * size] = unit(l, name).reshape(-1)
    r["weights"] = weights
    r["experts"] = np.concatenate([a["peer_u"], a["peer_v"]], axis=2).reshape(L * NEXP, 2 * D)
    r["gains"] = np.concatenate([a[n] for n in ("g_kv_lora", "g_q_lora", "g_qk_a_q", "g_qk_a_k", "g_v_b", "g_qk_c_q", "g_qk_c_k", "sink_c")], axis=1)
    r["b_mod"] = a["b_mod"]
    r["g_norm"] = np.concatenate([a["g_attn_norm"], a["g_ffn_norm"]], axis=1)
    r["b_s"] = np.ascontiguousarray(a["b_s_b"].transpose(0, 2, 1))
    r["ctx_kT"] = np.ascontiguousarray(a["cache_swa_k"][0].transpose(0, 3, 2, 1))
    r["ctx_v"] = np.ascontiguousarray(a["cache_swa_v"][0].reshape(L, 2, P, CKV * CD).transpose(0, 2, 1, 3))
    r["ctx_ckvT"] = np.ascontiguousarray(a["cache_mla_ckv"][0].reshape(L, 2 * P, 2, P).transpose(0, 3, 2, 1))
    r["ctx_kr"] = np.ascontiguousarray(a["cache_mla_krope"][0].reshape(L, 2, P, ROPE).transpose(0, 2, 1, 3).reshape(L, P, 2 * ROPE))
    r["keysT"] = np.ascontiguousarray(a["peer_keys"].reshape(L, 16, P, P).transpose(0, 3, 1, 2))
    cond = np.concatenate([a["c_ctx"][None], a["c"]], axis=0)
    r["cond"] = np.ascontiguousarray(cond.reshape(2, DK, P).transpose(2, 1, 0))
    r.update(shape_constants())
    return r


def shape_constants():
    import numpy as np

    q, k = np.arange(P)[:, None], np.arange(P)[None, :]
    mask = np.stack([np.where(k >= q, 0.0, NEG), np.where(k <= q, 0.0, NEG)], axis=1).astype(np.float32)
    pos = np.arange(4 * P)
    row, col = (pos // 64).astype(np.float32), (pos % 64).astype(np.float32)
    parts = []
    for dim in (ROPE, CD):
        quarter = dim // 4
        inv = (np.float32(10000.0) ** (-np.arange(quarter, dtype=np.float32) / np.float32(quarter))).astype(np.float32)
        ang = np.concatenate([row[:, None] * inv, col[:, None] * inv], axis=-1)
        parts += [np.cos(ang), np.sin(ang)]
    rope = np.concatenate(parts, axis=1).astype(np.float32).reshape(4, P, 96).transpose(1, 0, 2)
    return {"ident": np.eye(P, dtype=np.float32), "mask": mask, "rope": np.ascontiguousarray(rope)}


_OUTS = {
    "y_prompt": (1, 128, 1024), "y_sample": (1, 512, 1024), "new_mla_ckv": (1, 2, 128, 256),
    "new_mla_krope": (1, 2, 128, 32), "new_swa_k": (1, 2, 128, 2, 64), "new_swa_v": (1, 2, 128, 2, 64),
}


def kernel(**inputs):
    import concourse.bacc as _bacc
    from concourse.bass_utils import run_bass_kernel_spmd as _run

    nc = _bacc.Bacc("TRN2", target_bir_lowering=False, num_devices=1)
    arrays = lay_out(inputs)
    ins = {n: nc.dram_tensor(f"in_{n}", v.shape, mybir.dt.from_np(v.dtype), kind="ExternalInput").ap() for n, v in arrays.items()}
    outs = {n: nc.dram_tensor(f"out_{n}", s, F32, kind="ExternalOutput").ap() for n, s in _OUTS.items()}
    build(nc, ins, outs)
    r = _run(nc, [{f"in_{n}": v for n, v in arrays.items()}], core_ids=[0])
    return tuple(r.results[0][f"out_{n}"] for n in _OUTS)
```
